# Optimizing a Trainium2 kernel written in Bass

```python
import jax
import jax.numpy as jnp
from jax import lax
import numpy as np

D_MODEL = 1024
BATCH = 1
SEQ = 512
DEPTH = 1
DEC_BATCH = 8
DEC_SEQ = 4
PAST_LEN = 2048
PAGE_SIZE = 128

D_MIX = D_MODEL
NSA_WIDTH = D_MIX // 2
GM_WIDTH = D_MIX - NSA_WIDTH
HEAD_DIM = 64
N_HEADS = NSA_WIDTH // HEAD_DIM
N_KV = 2
HPG = N_HEADS // N_KV
KV_WIDTH = N_KV * HEAD_DIM
L_BLK = 64
N_SEL = 16
WINDOW = 512
WIN_QBLK = 128
SEL_QBLK = 16
CMP_HIDDEN = 2 * HEAD_DIM
GM_DIM = 64
GM_GROUPS = GM_WIDTH // GM_DIM
CHUNK = 128
N_EGROUPS = 4
EXPERTS_PER_GROUP = 4
N_EXPERTS = N_EGROUPS * EXPERTS_PER_GROUP
TOP_K = 2
EXPERT_HIDDEN = 512
N_PROJ = NSA_WIDTH + 6 * KV_WIDTH + 3 * N_HEADS + 2 * GM_WIDTH
EPS = 1e-6
NEG_INF = -1e30

kernel_name = 'hymba_gmlp_nsa_hmoe_step'

def _rms(x, g):
    xf = x.astype(jnp.float32)
    y = xf * lax.rsqrt(jnp.mean(xf * xf, axis=-1, keepdims=True) + EPS)
    return (y * g.astype(jnp.float32)).astype(x.dtype)

def _alibi_slopes():
    h = jnp.arange(1, N_HEADS + 1, dtype=jnp.float32)
    return jnp.exp2(-8.0 * h / N_HEADS).reshape(N_KV, HPG)

def _masked_softmax(s, mask):
    p = jax.nn.softmax(jnp.where(mask, s, NEG_INF), axis=-1)
    return jnp.where(mask, p, 0.0)

def _split_proj(p):
    sizes = [NSA_WIDTH, 2 * KV_WIDTH, 2 * KV_WIDTH, 2 * KV_WIDTH, 3 * N_HEADS, GM_WIDTH, GM_WIDTH]
    cuts = [int(c) for c in np.cumsum(sizes)[:-1]]
    q, kvc, kvs, kvw, gt, u, v = jnp.split(p, cuts, axis=-1)
    lead = p.shape[:-1]
    q = q.reshape(*lead, N_KV, HPG, HEAD_DIM)
    kvc = kvc.reshape(*lead, 2, N_KV, HEAD_DIM)
    kvs = kvs.reshape(*lead, 2, N_KV, HEAD_DIM)
    kvw = kvw.reshape(*lead, 2, N_KV, HEAD_DIM)
    gates = jax.nn.sigmoid(gt.astype(jnp.float32)).reshape(*lead, 3, N_KV, HPG)
    return q, kvc, kvs, kvw, gates, u, v

def _compress(blocks, pe, w1, w2):
    B, NB = blocks.shape[:2]
    x = blocks + jnp.transpose(pe, (1, 0, 2))[:, :, None, :]
    x = jnp.transpose(x, (0, 1, 3, 4, 2, 5)).reshape(B, NB, 2, N_KV, L_BLK * HEAD_DIM)
    h = jax.nn.gelu(jnp.einsum('bnckf,cfh->bnckh', x, w1))
    return jnp.einsum('bnckh,che->bncke', h, w2)

def _cmp_attention(qg, t, kc, vc, key_pos, slopes):
    s = jnp.einsum('btghd,bngd->bghtn', qg, kc).astype(jnp.float32) * HEAD_DIM ** -0.5
    dist = t[:, None] - key_pos[None, :]
    s = s - slopes[None, :, :, None, None] * dist.astype(jnp.float32)
    p = _masked_softmax(s, dist >= 0)
    o = jnp.einsum('bghtn,bngd->btghd', p, vc.astype(jnp.float32))
    return o, jnp.sum(p, axis=2)

def _select_blocks(imp, t, n_blocks):
    cand = jnp.arange(n_blocks)[None, :] < (t // L_BLK)[:, None]
    score = jnp.where(cand, imp, -1.0)
    val, idx = lax.top_k(score, min(N_SEL - 1, n_blocks))
    return jnp.swapaxes(idx, 1, 2).astype(jnp.int32), jnp.swapaxes(val, 1, 2) >= 0.0

def _sel_core(qg, t, ks, vs, pos_sel, valid, kc, vc, pos_cur, slopes):
    B, Q, G, K, L = ks.shape[:5]
    scale = HEAD_DIM ** -0.5
    sl = slopes[None, None, :, :, None]
    s_sel = jnp.einsum('bqghd,bqgkld->bqghkl', qg, ks).astype(jnp.float32).reshape(B, Q, G, HPG, K * L) * scale
    d_sel = (t[None, :, None, None, None] - pos_sel).reshape(B, Q, G, 1, K * L)
    s_sel = s_sel - sl * d_sel.astype(jnp.float32)
    m_sel = jnp.broadcast_to(jnp.repeat(valid, L, axis=-1)[:, :, :, None, :], s_sel.shape)
    s_cur = jnp.einsum('bqghd,blgd->bqghl', qg, kc).astype(jnp.float32) * scale
    d_cur = t[:, None] - pos_cur[None, :]
    s_cur = s_cur - sl * d_cur[None, :, None, None, :].astype(jnp.float32)
    m_cur = jnp.broadcast_to((d_cur >= 0)[None, :, None, None, :], s_cur.shape)
    p = _masked_softmax(jnp.concatenate([s_sel, s_cur], -1), jnp.concatenate([m_sel, m_cur], -1))
    p_sel = p[..., :K * L].reshape(B, Q, G, HPG, K, L)
    p_cur = p[..., K * L:]
    return (jnp.einsum('bqghkl,bqgkld->bqghd', p_sel, vs.astype(jnp.float32))
            + jnp.einsum('bqghl,blgd->bqghd', p_cur, vc.astype(jnp.float32)))

def _win_core(qg, t, kw, vw, pos_k, slopes):
    s = jnp.einsum('bqghd,bkgd->bqghk', qg, kw).astype(jnp.float32) * HEAD_DIM ** -0.5
    d = t[:, None] - pos_k[None, :]
    mask = (d >= 0) & (d <= WINDOW) & (pos_k >= 0)[None, :]
    s = s - slopes[None, None, :, :, None] * d[None, :, None, None, :].astype(jnp.float32)
    p = _masked_softmax(s, mask[None, :, None, None, :])
    return jnp.einsum('bqghk,bkgd->bqghd', p, vw.astype(jnp.float32))

def _merge_branches(gates, o_cmp, o_sel, o_win):
    g = gates[..., None]
    return g[:, :, 0] * o_cmp + g[:, :, 1] * o_sel + g[:, :, 2] * o_win

def _nsa_prompt(q, kv_cmp, kv_sel, kv_win, gates, pe_cmp, w_cmp1, w_cmp2, slopes):
    B, T = q.shape[:2]
    nb = T // L_BLK
    t = jnp.arange(T, dtype=jnp.int32)
    off = jnp.arange(L_BLK, dtype=jnp.int32)
    comp = _compress(kv_cmp.reshape(B, nb, L_BLK, 2, N_KV, HEAD_DIM), pe_cmp, w_cmp1, w_cmp2)
    blk_end = (jnp.arange(nb, dtype=jnp.int32) + 1) * L_BLK - 1
    o_cmp, imp = _cmp_attention(q, t, comp[:, :, 0], comp[:, :, 1], blk_end, slopes)
    idx, valid = _select_blocks(imp, t, nb)
    kb = kv_sel[:, :, 0].reshape(B, nb, L_BLK, N_KV, HEAD_DIM)
    vb = kv_sel[:, :, 1].reshape(B, nb, L_BLK, N_KV, HEAD_DIM)
    nq = T // SEL_QBLK

    def qblocks(a):
        return jnp.moveaxis(a.reshape(B, nq, SEL_QBLK, *a.shape[2:]), 1, 0)

    b_ix = jnp.arange(B)[:, None, None, None]
    g_ix = jnp.arange(N_KV)[None, None, :, None]

    def sel_step(args):
        i, qi, idx_i, val_i = args
        c = (i * SEL_QBLK) // L_BLK
        ti = i * SEL_QBLK + jnp.arange(SEL_QBLK, dtype=jnp.int32)
        ks = kb[b_ix, idx_i, :, g_ix]
        vs = vb[b_ix, idx_i, :, g_ix]
        kc = lax.dynamic_index_in_dim(kb, c, axis=1, keepdims=False)
        vc = lax.dynamic_index_in_dim(vb, c, axis=1, keepdims=False)
        return _sel_core(qi, ti, ks, vs, idx_i[..., None] * L_BLK + off, val_i, kc, vc, c * L_BLK + off, slopes)

    o_sel = lax.map(sel_step, (jnp.arange(nq, dtype=jnp.int32), qblocks(q), qblocks(idx), qblocks(valid)))
    o_sel = jnp.moveaxis(o_sel, 0, 1).reshape(B, T, N_KV, HPG, HEAD_DIM)
    pad = [(0, 0), (WINDOW, 0), (0, 0), (0, 0)]
    kwp = jnp.pad(kv_win[:, :, 0], pad)
    vwp = jnp.pad(kv_win[:, :, 1], pad)
    nw = T // WIN_QBLK
    span = WINDOW + WIN_QBLK

    def win_step(args):
        i, qi = args
        start = i * WIN_QBLK
        ki = lax.dynamic_slice_in_dim(kwp, start, span, axis=1)
        vi = lax.dynamic_slice_in_dim(vwp, start, span, axis=1)
        ti = start + jnp.arange(WIN_QBLK, dtype=jnp.int32)
        pos = start - WINDOW + jnp.arange(span, dtype=jnp.int32)
        return _win_core(qi, ti, ki, vi, pos, slopes)

    qw = jnp.moveaxis(q.reshape(B, nw, WIN_QBLK, N_KV, HPG, HEAD_DIM), 1, 0)
    o_win = lax.map(win_step, (jnp.arange(nw, dtype=jnp.int32), qw))
    o_win = jnp.moveaxis(o_win, 0, 1).reshape(B, T, N_KV, HPG, HEAD_DIM)
    return _merge_branches(gates, o_cmp, o_sel, o_win).astype(q.dtype).reshape(B, T, NSA_WIDTH)

def _nsa_sample(q, kv_cmp, kv_sel, kv_win, gates, cache_cmp, cache_sel, win_buf, page_table,
                pe_cmp, w_cmp1, w_cmp2, slopes):
    Bd, S = q.shape[:2]
    past = page_table.shape[1] * PAGE_SIZE
    nb = past // L_BLK
    t = past + jnp.arange(S, dtype=jnp.int32)
    off = jnp.arange(L_BLK, dtype=jnp.int32)
    past_cmp = cache_cmp[page_table].reshape(Bd, nb, L_BLK, 2, N_KV, HEAD_DIM)
    comp = _compress(past_cmp, pe_cmp, w_cmp1, w_cmp2)
    blk_end = (jnp.arange(nb, dtype=jnp.int32) + 1) * L_BLK - 1
    o_cmp, imp = _cmp_attention(q, t, comp[:, :, 0], comp[:, :, 1], blk_end, slopes)
    idx, valid = _select_blocks(imp, t, nb)
    bpp = PAGE_SIZE // L_BLK
    b_ix = jnp.arange(Bd)[:, None, None, None]
    g_ix = jnp.arange(N_KV)[None, None, :, None]
    phys = page_table[b_ix, idx // bpp] * bpp + idx % bpp
    pool_blocks = cache_sel.reshape(-1, L_BLK, 2, N_KV, HEAD_DIM)
    rows = pool_blocks[phys, :, :, g_ix]
    o_sel = _sel_core(q, t, rows[..., 0, :], rows[..., 1, :], idx[..., None] * L_BLK + off, valid,
                      kv_sel[:, :, 0], kv_sel[:, :, 1], t, slopes)
    wb = win_buf.shape[1]
    kw = jnp.concatenate([win_buf[:, :, 0], kv_win[:, :, 0]], axis=1)
    vw = jnp.concatenate([win_buf[:, :, 1], kv_win[:, :, 1]], axis=1)
    pos = past - wb + jnp.arange(wb + S, dtype=jnp.int32)
    o_win = _win_core(q, t, kw, vw, pos, slopes)
    return _merge_branches(gates, o_cmp, o_sel, o_win).astype(q.dtype).reshape(Bd, S, NSA_WIDTH)

def _gmlp(u_raw, v_raw, ln_g, ln_b, w_s, b_s):
    B, T = u_raw.shape[:2]
    u = jax.nn.gelu(u_raw).reshape(B, T, GM_GROUPS, GM_DIM)
    vf = jax.nn.gelu(v_raw.astype(jnp.float32)).reshape(B, T, GM_GROUPS, GM_DIM)
    mu = jnp.mean(vf, axis=-1, keepdims=True)
    var = jnp.mean(jnp.square(vf - mu), axis=-1, keepdims=True)
    vn = ((vf - mu) * lax.rsqrt(var + EPS) * ln_g + ln_b).astype(u_raw.dtype)
    n = min(T, CHUNK)
    vc = vn.reshape(B, T // n, n, GM_GROUPS, GM_DIM)
    ws = jnp.tril(w_s[:, :n, :n])
    mixed = jnp.einsum('gts,bcsgd->bctgd', ws, vc) + jnp.transpose(b_s[:, :n])[None, None, :, :, None]
    out = u * mixed.reshape(B, T, GM_GROUPS, GM_DIM)
    return out.reshape(B, T, GM_WIDTH), vn

def _mix_out(o_nsa, o_gm, g, w_out):
    o = jnp.concatenate([_rms(o_nsa, g[:NSA_WIDTH]), _rms(o_gm, g[NSA_WIDTH:])], axis=-1)
    return o @ w_out

def _hier_moe(x, w_rg, b_rg, w_re, b_re, w_gate, w_up, w_down):
    lead = x.shape[:-1]
    xt = x.reshape(-1, D_MODEL)
    n = xt.shape[0]
    rows = jnp.arange(n)
    lg = (xt @ w_rg).astype(jnp.float32) + b_rg
    grp = jnp.argmax(lg, axis=-1)
    g_gate = jax.nn.softmax(lg, axis=-1)[rows, grp][:, None]
    le = ((xt @ w_re).astype(jnp.float32) + b_re).reshape(n, N_EGROUPS, EXPERTS_PER_GROUP)[rows, grp]
    top_p, top_i = lax.top_k(jax.nn.softmax(le, axis=-1), TOP_K)
    w = g_gate * top_p / jnp.sum(top_p, axis=-1, keepdims=True)
    eid = grp[:, None] * EXPERTS_PER_GROUP + top_i
    combine = jnp.zeros((n, N_EXPERTS), jnp.float32).at[rows[:, None], eid].add(w)
    y = jnp.zeros((n, D_MODEL), jnp.float32)
    for e in range(N_EXPERTS):
        h = jax.nn.silu(xt @ w_gate[e]) * (xt @ w_up[e])
        y = y + combine[:, e:e + 1] * (h @ w_down[e]).astype(jnp.float32)
    return y.astype(x.dtype).reshape(*lead, D_MODEL)

def setup_inputs(seed: int = 0) -> dict:
    key = jax.random.key(seed)
    ks = iter(jax.random.split(key, 32))

    def nrm(shape, scale):
        return jax.random.normal(next(ks), shape, jnp.float32) * scale

    n_pages = PAST_LEN // PAGE_SIZE
    n_used = DEC_BATCH * n_pages
    n_pool = n_used + max(1, n_used // 4)
    wbuf = min(WINDOW, PAST_LEN)
    pool_shape = (DEPTH, n_pool, PAGE_SIZE, 2, N_KV, HEAD_DIM)
    x_prompt = nrm((BATCH, SEQ, D_MODEL), 1.0)
    x_sample = nrm((DEC_BATCH, DEC_SEQ, D_MODEL), 1.0)
    cache_cmp_kv = nrm(pool_shape, 1.0)
    cache_sel_kv = nrm(pool_shape, 1.0)
    state_win_kv = nrm((DEPTH, DEC_BATCH, wbuf, 2, N_KV, HEAD_DIM), 1.0)
    perm = jax.random.permutation(next(ks), n_pool)[:n_used].astype(jnp.int32)
    page_table = perm.reshape(DEC_BATCH, n_pages)
    return {
        'x_prompt': x_prompt,
        'x_sample': x_sample,
        'cache_cmp_kv': cache_cmp_kv,
        'cache_sel_kv': cache_sel_kv,
        'state_win_kv': state_win_kv,
        'page_table': page_table,
        'norm1_g': 1.0 + nrm((DEPTH, D_MODEL), 0.02),
        'w_in': nrm((DEPTH, D_MODEL, N_PROJ), D_MODEL ** -0.5),
        'pe_cmp': nrm((DEPTH, 2, L_BLK, HEAD_DIM), 0.5),
        'w_cmp1': nrm((DEPTH, 2, L_BLK * HEAD_DIM, CMP_HIDDEN), (L_BLK * HEAD_DIM) ** -0.5),
        'w_cmp2': nrm((DEPTH, 2, CMP_HIDDEN, HEAD_DIM), CMP_HIDDEN ** -0.5),
        'gm_ln_g': 1.0 + nrm((DEPTH, GM_GROUPS, GM_DIM), 0.02),
        'gm_ln_b': nrm((DEPTH, GM_GROUPS, GM_DIM), 0.02),
        'w_spatial': nrm((DEPTH, GM_GROUPS, CHUNK, CHUNK), 0.5 * CHUNK ** -0.5),
        'b_spatial': 1.0 + nrm((DEPTH, GM_GROUPS, CHUNK), 0.1),
        'out_norm_g': 1.0 + nrm((DEPTH, D_MIX), 0.02),
        'w_out': nrm((DEPTH, D_MIX, D_MODEL), D_MIX ** -0.5),
        'norm2_g': 1.0 + nrm((DEPTH, D_MODEL), 0.02),
        'w_router_group': nrm((DEPTH, D_MODEL, N_EGROUPS), D_MODEL ** -0.5),
        'b_router_group': nrm((DEPTH, N_EGROUPS), 0.01),
        'w_router_expert': nrm((DEPTH, D_MODEL, N_EXPERTS), D_MODEL ** -0.5),
        'b_router_expert': nrm((DEPTH, N_EXPERTS), 0.01),
        'w_gate_e': nrm((DEPTH, N_EXPERTS, D_MODEL, EXPERT_HIDDEN), D_MODEL ** -0.5),
        'w_up_e': nrm((DEPTH, N_EXPERTS, D_MODEL, EXPERT_HIDDEN), D_MODEL ** -0.5),
        'w_down_e': nrm((DEPTH, N_EXPERTS, EXPERT_HIDDEN, D_MODEL), EXPERT_HIDDEN ** -0.5),
        'final_norm_g': 1.0 + nrm((D_MODEL,), 0.02),
    }

def reference(x_prompt, x_sample, cache_cmp_kv, cache_sel_kv, state_win_kv, page_table,
              norm1_g, w_in, pe_cmp, w_cmp1, w_cmp2, gm_ln_g, gm_ln_b, w_spatial, b_spatial,
              out_norm_g, w_out, norm2_g, w_router_group, b_router_group, w_router_expert,
              b_router_expert, w_gate_e, w_up_e, w_down_e, final_norm_g):
    slopes = _alibi_slopes()
    xp = x_prompt
    xs = x_sample
    cmp_p, cmp_s, sel_p, sel_s, win_p, win_s, gm_s = [], [], [], [], [], [], []
    for l in range(DEPTH):
        q, kvc, kvs, kvw, gates, u, v = _split_proj(_rms(xp, norm1_g[l]) @ w_in[l])
        o_nsa = _nsa_prompt(q, kvc, kvs, kvw, gates, pe_cmp[l], w_cmp1[l], w_cmp2[l], slopes)
        o_gm, _ = _gmlp(u, v, gm_ln_g[l], gm_ln_b[l], w_spatial[l], b_spatial[l])
        xp = xp + _mix_out(o_nsa, o_gm, out_norm_g[l], w_out[l])
        xp = xp + _hier_moe(_rms(xp, norm2_g[l]), w_router_group[l], b_router_group[l], w_router_expert[l],
                            b_router_expert[l], w_gate_e[l], w_up_e[l], w_down_e[l])
        T = kvw.shape[1]
        cmp_p.append(kvc)
        sel_p.append(kvs)
        win_p.append(kvw[:, T - min(WINDOW, T):])
        q, kvc, kvs, kvw, gates, u, v = _split_proj(_rms(xs, norm1_g[l]) @ w_in[l])
        o_nsa = _nsa_sample(q, kvc, kvs, kvw, gates, cache_cmp_kv[l], cache_sel_kv[l], state_win_kv[l],
                            page_table, pe_cmp[l], w_cmp1[l], w_cmp2[l], slopes)
        o_gm, vn = _gmlp(u, v, gm_ln_g[l], gm_ln_b[l], w_spatial[l], b_spatial[l])
        xs = xs + _mix_out(o_nsa, o_gm, out_norm_g[l], w_out[l])
        xs = xs + _hier_moe(_rms(xs, norm2_g[l]), w_router_group[l], b_router_group[l], w_router_expert[l],
                            b_router_expert[l], w_gate_e[l], w_up_e[l], w_down_e[l])
        cmp_s.append(kvc)
        sel_s.append(kvs)
        win_s.append(kvw)
        gm_s.append(vn)
    y_prompt = _rms(xp, final_norm_g)
    y_sample = _rms(xs, final_norm_g)
    new_cmp_kv_prompt = jnp.stack(cmp_p)
    new_cmp_kv_sample = jnp.stack(cmp_s)
    new_sel_kv_prompt = jnp.stack(sel_p)
    new_sel_kv_sample = jnp.stack(sel_s)
    new_win_kv_prompt = jnp.stack(win_p)
    new_win_kv_sample = jnp.stack(win_s)
    new_gm_v_sample = jnp.stack(gm_s)
    return (y_prompt, y_sample, new_cmp_kv_prompt, new_cmp_kv_sample, new_sel_kv_prompt, new_sel_kv_sample,
            new_win_kv_prompt, new_win_kv_sample, new_gm_v_sample)


_drawn_inputs = setup_inputs


def setup_inputs(seed=0):
    import zlib

    import numpy as np

    out = dict(_drawn_inputs(seed))
    spreads = {}
    factors = {'gm_ln_g': 2.777,
     'gm_ln_b': 2.873,
     'out_norm_g': 2.851,
     'norm2_g': 3.555,
     'b_router_expert': 8.0,
     'final_norm_g': 2.756}
    for name, (base, spread) in spreads.items():
        noise = np.random.default_rng([zlib.crc32(name.encode()), seed]).standard_normal(out[name].shape)
        drawn = base * np.exp(spread * noise) if base else spread * noise
        out[name] = jnp.asarray(drawn.astype(out[name].dtype))
    for name, factor in factors.items():
        out[name] = (out[name] * factor).astype(out[name].dtype)
    return out
```

```python
from contextlib import ExitStack

import numpy as np

import concourse.bass as bass
from concourse import mybir

F32 = mybir.dt.float32
I32 = mybir.dt.int32
U32 = mybir.dt.uint32
ALU = mybir.AluOpType
ACT = mybir.ActivationFunctionType
AX = mybir.AxisListType.X

P = 128
D = 1024
KD = D // P
SEQ = 512
NB, NT = 8, 4
NS = NB * NT
TOK = SEQ + NS
PT = SEQ // P
TILES = PT + 1
ROWS = [P] * PT + [NS]
H, HD, G, HPG = 8, 64, 2, 4
PAST, PAGE, L = 2048, 128, 64
PAGES = PAST // PAGE
BLKS = PAST // L
PBLK = SEQ // L
NSEL = 15
WIN = 512
NPOOL = 160
W = 512
GM = 8
CUT = [(1816, 2328), (1304, 1816), (0, 512), (512, 1024), (1024, 1304)]
BLK_V, BLK_U, BLK_Q, BLK_KC, BLK_KW = range(5)
WIN_SLOT = (4, 5, 4, 5, 4)
SEL_SLOT = (2, 3, 5, 4)
NPROJ = 2328
E, EH = 16, 512
FE = EH // P
CAP = 128
PASSES = -(-TOK // CAP)
EPS = 1e-6
BIG = 1e30
FAR = 1 << 20
HALF = NB // 2
SLOT = 4096
CURW = NS
SELW = PAST + CURW
WINW = WIN + CURW

C_ID, C_ONE, C_TRI, C_HS = 0, 128, 256, 384
C_SG = 512
C_SO = C_SG + 256
C_HM = C_SO + 512
C_GM = C_HM + 24
C_PB = C_GM + 2
C_PM = C_PB + PT * 64
C_SB = C_PM + PT * 64
C_VM = C_SB + BLKS
C_WS = C_VM + H
C_IE = C_WS + NS
C_VT = C_IE + E
C_OF = C_VT + TILES
C_BL = C_OF + L
C_CU = C_BL + BLKS
C_WB = C_CU + CURW
C_ND = C_WB + WIN


def slopes():
    return np.exp2(-np.arange(1, H + 1, dtype=np.float64))


def constants():
    c = np.zeros((P, C_ND), np.float32)
    p = np.arange(P)
    c[:, C_ID:C_ID + P] = np.eye(P)
    c[:, C_ONE:C_ONE + P] = 1
    c[:, C_TRI:C_TRI + P] = p[:, None] <= p[None, :]
    b, g, h, t = p // 32, p // 16 % 2, p // 4 % 4, p % 4
    same = (b[:, None] == b) & (g[:, None] == g) & (t[:, None] == t)
    c[:, C_HS:C_HS + P] = same
    head = g * HPG + h
    slope = slopes()[head]
    for hf in range(2):
        token = (hf * HALF + b) * NT + t
        for r in range(P):
            c[token[r], C_SG + hf * P + r] = 1
            c[r, C_SO + (hf * H + head[r]) * NS + token[r]] = 1
    for br in range(3):
        c[p, C_HM + br * H + head] = 1
    c[p, C_GM + g] = 1
    for i in range(PT):
        for hh in range(H):
            at = i * 64 + hh * PBLK
            dist = (i * P + p)[:, None] - ((np.arange(PBLK) + 1) * L - 1)[None, :]
            c[:, C_PB + at:C_PB + at + PBLK] = np.where(dist >= 0, slopes()[hh] * dist, BIG)
            c[:, C_PM + at:C_PM + at + PBLK] = dist >= 0
    now = PAST + t
    c[:, C_SB:C_SB + BLKS] = slope[:, None] * (now[:, None] - ((np.arange(BLKS) + 1) * L - 1))
    c[p[:64], C_VM + p[:64] // PBLK] = 1
    q = np.arange(NS)
    c[:NS, C_WS:C_WS + NS] = (q[:, None] // NT == q // NT) & (q[:, None] <= q)
    c[:, C_IE:C_IE + E] = np.arange(E)
    for i in range(TILES):
        c[:ROWS[i], C_VT + i] = 1
    c[:, C_OF:C_OF + L] = -slope[:, None] * np.arange(L)
    c[:, C_BL:C_BL + BLKS] = slope[:, None] * (now[:, None] - L * np.arange(BLKS))
    back = t[:, None] - (q % NT)[None, :]
    mine = (q // NT)[None, :] == b[:, None]
    c[:, C_CU:C_CU + NS] = np.where(mine & (back >= 0), slope[:, None] * back, BIG)
    dist = now[:, None] - (PAST - WIN + np.arange(WIN))
    c[:, C_WB:C_WB + WIN] = np.where(dist <= WIN, slope[:, None] * dist, BIG)
    j = np.arange(SEQ)
    back = p[:, None] - (j[None, :] - (SEQ - P))
    alibi = np.stack([np.where(back >= 0, s * back, BIG) for s in slopes()], 1).astype(np.float32)
    i = np.arange(BLKS)
    earlier = (i[None, :] < i[:, None]).astype(np.float32).reshape(1, -1)
    return c, alibi, np.repeat(earlier, P, 0)


def hybrid_layer(nc, t, o):
    scratch_h2 = nc.dram_tensor("h2_rows", (TOK, D), F32, kind="Internal").ap()
    scratch_y = nc.dram_tensor("expert_rows", (E * CAP, D), F32, kind="Internal").ap()
    scratch_z = nc.dram_tensor("more_expert_rows", (E * (PASSES - 1) * CAP, D), F32, kind="Internal").ap()
    scratch_ix = nc.dram_tensor("slot_tokens", (PASSES * CAP * E, 1), I32, kind="Internal").ap()

    with ExitStack() as ctx:
        def sb(name, shape, dt=F32):
            return ctx.enter_context(nc.sbuf_tensor(name, shape, dt))

        sems = {}

        def sem(name):
            if name not in sems:
                sems[name] = ctx.enter_context(nc.semaphore(name))
            return sems[name]

        ring = sb("ring", [P, 6, SLOT])
        xr = sb("xr", [P, 5120])
        qT = sb("qT", [P, HPG, TOK])
        ksT = sb("ksT", [P, TOK])
        kwT = sb("kwT", [P, TOK])
        kvn = sb("kvn", [P, TILES, W])
        ugr = sb("ugr", [P, TILES * W])
        vnr = sb("vnr", [P, TILES * W])
        tabs = sb("tabs", [P, 4096])
        work = sb("work", [P, 3072])
        cst = sb("cst", [P, C_ND])
        gates = sb("gates", [P, TILES, 24])
        qbd = sb("qbd", [P, NB, 32])
        kcs = sb("kcs", [P, NB * BLKS])
        kcp = sb("kcp", [P, PBLK])
        vcp = sb("vcp", [64, W])
        w2 = sb("w2", [P, 2, HD])
        pe = sb("pe", [P, 2, 32])
        peb = sb("peb", [P, 2])
        vec = sb("vec", [P, 2 * KD])
        pages = sb("pages", [1, P], I32)
        small = sb("small", [P, 160])
        osm = sb("osm", [P, 2, HD])
        rt = sb("rt", [P, 512])
        ints = sb("ints", [P, 96], I32)
        empty = tabs[:, 3584:3584 + PASSES * CAP * E // P].bitcast(I32)
        slot_tokens = qbd[:, :, :].rearrange("p b n -> p (b n)")[:, 0:PASSES * E].bitcast(I32)

        def vcs(b):
            r = 32 + 32 * (b // HALF)
            return kvn[r:r + 32, PT, P * (b % HALF):P * (b % HALF) + P]

        pb = [ctx.enter_context(nc.psum_tensor(f"pb{i}", [P, 512], F32)) for i in range(8)]

        ident = cst[:, C_ID:C_ID + P]
        ones = cst[:, C_ONE:C_ONE + P]
        xT = xr[:, 0:KD * TOK].rearrange("p (k n) -> p k n", k=KD)
        sq = [(ugr, vnr)[k // 4][:, (k % 4) * TOK:(k % 4 + 1) * TOK] for k in range(KD)]
        ug = ugr[:, :].rearrange("p (i n) -> p i n", i=TILES)
        vn = vnr[:, :].rearrange("p (i n) -> p i n", i=TILES)
        ov = vn
        rb = work[:, 2048:2048 + TOK]
        w1 = ring[:, 0:2, :].rearrange("p s (l h) -> p s l h", h=P)
        hc = work[:, 0:1024].rearrange("p (c n) -> p c n", c=2)
        xp = work[:, 1024:2048].rearrange("p (c l n) -> p c l n", c=2, l=32)
        stg = work[:, 2048:3072].rearrange("p (s n) -> p s n", s=2)
        stk = work[:, 2048:3072].rearrange("p (s n) -> p s n", s=4)
        hp = small[:, 0:32].rearrange("p (c n) -> p c n", c=2)
        hrep = small[:, 32:96]
        lng = tabs[:, 0:512]
        lnb = tabs[:, 512:1024]
        wst = tabs[:, 1024:2048].rearrange("p (g n) -> p g n", g=GM)
        lsq = tabs[:, 2048:2560]
        wss = tabs[0:NS, 2560:2816].rearrange("p (g n) -> p g n", g=GM)
        bst = tabs[:, 2816:2824]
        bss = tabs[0:NS, 2824:2832]
        lst = tabs[:, 2832:2872]

        psel = xr[:, 0:SELW]
        ptsel = xr[:, SELW:SELW + PAST].rearrange("p (c n) -> p c n", c=PAGES)
        pwin = xr[:, SELW + PAST:SELW + PAST + WINW]
        ptwin = work[:, 0:512].rearrange("p (c n) -> p c n", c=4)
        ptcs = work[0:32, 512:640]
        ptcw = work[0:32, 640:768]
        ptc = [work[32 * (hf + 1):32 * (hf + 2), 768:896] for hf in range(2)]
        rank = work[:, 1024:2048].rearrange("p (a b) -> p a b", a=BLKS)
        earlier = work[:, 2048:3072]
        sb3 = [work[:, 512 * k:512 * (k + 1)] for k in range(3)]
        pts = [work[:, 1536 + 512 * k:2048 + 512 * k] for k in range(2)]
        alibi = tabs[:, :].rearrange("p (h n) -> p h n", h=H)
        pcT = rt[0:64, 0:128]
        branch = work[:, 2560:3072]

        mixT = [work[:, 1024 * k:1024 * (k + 1)].rearrange("p (c n) -> p c n", c=KD) for k in range(2)]
        x2 = xr[:, :].rearrange("p (i n) -> p i n", i=TILES)
        g2 = tabs[:, 0:1024]
        h2 = [tabs[:, 1024 * (1 + k):1024 * (2 + k)] for k in range(2)]
        h2T = tabs[:, 3072:4096].rearrange("p (c n) -> p c n", c=KD)
        wr = work[:, 2048:2208].rearrange("p (c n) -> p c n", c=KD)
        br = work[:, 2208:2228]
        xe = [ugr[:, 1024 * k:1024 * (k + 1)] for k in range(2)]
        xeT = [vnr[:, 1024 * k:1024 * (k + 1)].rearrange("p (c n) -> p c n", c=KD) for k in range(2)]
        kvf = kvn[:, :, :].rearrange("p i n -> p (i n)")
        ye = [kvf[:, 1024 * k:1024 * (k + 1)] for k in range(2)]
        qf = qT[:, :, :].rearrange("p i n -> p (i n)")
        he = [qf[:, 512 * k:512 * (k + 1)].rearrange("p (f n) -> p f n", f=FE) for k in range(2)]
        sg = [qf[:, 1024 + 512 * k:1024 + 512 * (k + 1)].rearrange("p (f n) -> p f n", f=FE) for k in range(2)]
        WG, WU, WD = (2, 5), (3, 0), (4, 1)
        yg = [ring[:, 2 + n // 4, 1024 * (n % 4):1024 * (n % 4 + 1)] for n in range(2 * TILES)]
        gf = ring[:, 5, 0:1024]

        def after(eng, name, value):
            if not isinstance(value, int) or value > 0:
                eng.wait_ge(sem(name), value)

        def expert_units(b, first, eng, last):
            def unit(e, half, par):
                return e, b * E + e, par, b * (E // 2) + half

            first(*unit(0, 0, 0))
            first(*unit(1, 0, 1))
            last(*unit(0, 0, 0))
            first(*unit(2, 1, 0))
            last(*unit(1, 0, 1))
            with eng.Fori(1, E // 2 - 1) as m:
                first(*unit(2 * m + 1, m, 1))
                last(*unit(2 * m, m, 0))
                first(*unit(2 * m + 2, m + 1, 0))
                last(*unit(2 * m + 1, m, 1))
            first(*unit(E - 1, E // 2 - 1, 1))
            last(*unit(E - 2, E // 2 - 1, 0))
            last(*unit(E - 1, E // 2 - 1, 1))

        def gsel(hh):
            return slice(64 * (hh // HPG), 64 * (hh // HPG) + 64), hh % HPG

        def load_pages(eng, first, count, table, dst, name, at_once):
            def turn(j):
                for k in range(at_once):
                    page = eng.value_load(pages[0:1, bass.ds(j + first + k, 1)], min_val=0, max_val=NPOOL - 1)
                    eng.dma_start(dst[:, bass.ds(j * 256 + k * 256, 256)],
                                  table[bass.ds(page, 1), :, :].rearrange("o p n -> (o p) n")
                                  ).then_inc(sem(name), 16)

            if count == at_once:
                turn(0)
            else:
                with eng.Fori(0, count // at_once) as m:
                    turn(m * at_once)

        LATE = 3 * TILES

        units = [(i, br_, hh) for i in range(PT) for br_ in range(2) for hh in range(H)]
        CHUNKS = [range(0, 32), range(32, 64)]

        block = ctx.enter_context(nc.Block())

        @block.sync
        def _(sp):
            def load(dst, src, name):
                sp.dma_start(dst, src).then_inc(sem(name), 16)

            def w_in(nb):
                a, b = CUT[nb]
                dst = ring[:, WIN_SLOT[nb], 0:KD * (b - a)].rearrange("p (k n) -> p k n", k=KD)
                load(dst, t["w_in"][:, a:b].rearrange("(k p) n -> p k n", p=P), "win_in%d" % (nb % 2))

            cmp_dst = ring[:, 2:4, :].rearrange("p s n -> p (s n)")
            load(xr[:, 0:KD * TOK], t["xT"], "x_in")
            load(cst[:, :], t["consts"], "cst_in")
            load(pages[:, :], t["pages"], "pages_in")
            load(vec[:, 0:KD], t["g1"], "pe_in")
            w_in(BLK_V)
            load(vec[:, KD:2 * KD], t["gout"], "pe_in")
            load(pe[:, :, :], t["pe"], "pe_in")
            load(w2[:, :, :], t["w2"], "pe_in")
            load(ring[:, 0:2, :], t["w1"], "w1_in")
            sp.wait_ge(sem("pages_in"), 16)
            load_pages(sp, 0, PAGES, t["cmp_pages"], cmp_dst, "cmp_in_sp", 4)
            w_in(BLK_U)
            load(lng, t["ln_g"].to_broadcast([P, 512]), "gm_in")
            load(lnb, t["ln_b"].to_broadcast([P, 512]), "gm_in")
            load(tabs[:, 1024:2048], t["ws_t"], "gm_in")
            load(tabs[0:NS, 2560:2816], t["ws_s"], "gm_in")
            load(bst, t["bs_t"], "gm_in")
            load(bss, t["bs_s"], "gm_in")
            for s in range(1, 4):
                sp.wait_ge(sem("proj_done"), TILES * s)
                w_in(s + 1)
                sp.wait_ge(sem("cmp_mm"), 2 * s)
                first = 32 * s
                load_pages(sp, first, PAGES, t["cmp_pages"], cmp_dst, "cmp_in_sp", 4)
                if s == 3:
                    rest = 2 * PAGES - PAGES - LATE
                    load_pages(sp, first + 2 * PAGES - rest, rest, t["cmp_pages"],
                               cmp_dst[:, (2 * PAGES - rest) * 256:], "cmp_in_sp", rest)

            def selected(hf):
                for q in range(0, HALF, 2):
                    if hf == 0:
                        if q == 0:
                            sp.wait_ge(sem("cmp_mm"), 8)
                        else:
                            sp.wait_ge(sem("proj_done"), TILES * 4)
                    elif q == 0:
                        sp.wait_ge(sem("samp_pv"), 1)
                    load_pages(sp, PAGES * (hf * HALF + q), PAGES, t["sel_pages"], ring[:, SEL_SLOT[q], :],
                               "sel_in%d" % q, 4)
                    if q == 0:
                        if hf == 0:
                            sp.wait_ge(sem("pcmp_h"), 2)
                        load(ring[:, hf, :].rearrange("p (q n) -> p q n", q=HALF),
                             t["win"][hf * HALF:(hf + 1) * HALF].rearrange("q p n -> p q n"), "wst_in%d" % hf)

            selected(0)
            sp.wait_ge(sem("slots_empty"), 16)
            sp.wait_ge(sem("earlier_free"), 1)
            sp.wait_ge(sem("kvc_first"), 16)
            sp.wait_ge(sem("kvc_out"), 16 * (TILES - 1))
            load(earlier, t["earlier"], "earlier_in")
            sp.wait_ge(sem("gm_done"), 1)
            load(tabs[:, :], t["alibi"], "alibi_in")
            selected(1)
            sp.wait_ge(sem("earlier_free"), 2)
            load(earlier, t["earlier"], "earlier_in")
            sp.wait_ge(sem("samp_pv"), 2)
            load(ring[:, 0:2, :].rearrange("p s n -> p (s n)").rearrange("p (k n) -> p k n", k=KD),
                 t["w_out"].rearrange("(k p) n -> p k n", p=P), "wout_in")
            for i in range(TILES):
                load(x2[0:ROWS[i], i, :], t["x"][i * P:i * P + ROWS[i], :], "xnat_in")
            sp.wait_ge(sem("attn_done"), 1)
            load(wr, t["w_router"], "router_in")
            load(br, t["b_router"].to_broadcast([P, 20]), "router_in")
            load(g2, t["g2"].to_broadcast([P, D]), "router_in")

            def slab(name, e):
                if isinstance(e, int):
                    return t[name][e]
                return t[name][bass.ds(e, 1), :, :].rearrange("o p n -> (o p) n")

            def gate(e, n, par, turn):
                after(sp, "u_mm", n - 1)
                load(ring[:, WG[par], :], slab("w_gate", e), "wg_in%d" % par)

            def up(e, n, par, turn):
                after(sp, "u_mm", n - 1)
                load(ring[:, WU[par], :], slab("w_up", e), "wu_in%d" % par)

            def gate_up(e, n, par, turn):
                gate(e, n, par, turn)
                up(e, n, par, turn)

            def down(e, n, par, turn):
                after(sp, "y_mm", 2 * n - 2)
                load(ring[:, WD[par], :], slab("w_down", e), "wd_in%d" % par)

            gate_up(0, 0, 0, 0)
            down(0, 0, 0, 0)
            gate(1, 1, 1, 0)
            sp.wait_ge(sem("out_mm"), 2 * TILES)
            up(1, 1, 1, 0)
            gate_up(2, 2, 0, 1)
            down(1, 1, 1, 0)
            with sp.Fori(1, E // 2 - 1) as m:
                gate_up(2 * m + 1, 2 * m + 1, 1, m)
                down(2 * m, 2 * m, 0, m)
                gate_up(2 * m + 2, 2 * m + 2, 0, m + 1)
                down(2 * m + 1, 2 * m + 1, 1, m)
            gate_up(E - 1, E - 1, 1, E // 2 - 1)
            down(E - 2, E - 2, 0, E // 2 - 1)
            down(E - 1, E - 1, 1, E // 2 - 1)
            sp.wait_ge(sem("flag_ready"), 1)
            more = sp.value_load(ints[0:1, 80:81], min_val=0, max_val=1)
            with sp.If(more != 0):
                with sp.Fori(1, PASSES) as b:
                    expert_units(b, gate_up, sp, down)
            sp.wait_ge(sem("y_all"), 1)
            load(gf, t["gf"].to_broadcast([P, D]), "gf_in")
            for i in range(TILES):
                sp.wait_ge(sem("out_ready"), i + 1)
                dst = o[0][i * P:(i + 1) * P, :] if i < PT else o[1]
                sp.dma_start(dst, yg[2 * i][0:ROWS[i], :]).then_inc(sem("stored"), 16)
            sp.wait_ge(sem("stored"), 16 * TILES)

        @block.tensor
        def _(te):
            def mm(out, lhsT, rhs, start=True, stop=True):
                return nc.tensor.matmul(out, lhsT, rhs, start=start, stop=stop)

            te.wait_ge(sem("cst_in"), 16)
            for k in range(KD):
                te.wait_ge(sem("sq_ready"), k + 1)
                for n in range(2):
                    ins = mm(pb[4 + n][:, 0:272], ones, sq[k][:, 272 * n:272 * (n + 1)], k == 0, k == KD - 1)
            ins.then_inc(sem("ss_mm"), 1)

            def position_bias():
                te.wait_ge(sem("pe_in"), 64)
                te.wait_ge(sem("w1_in"), 16)
                for c in range(2):
                    for l in range(32):
                        ins = mm(pb[7][:, c:c + 1], w1[:, c, l, :], pe[:, c, l:l + 1], l == 0, l == 31)
                ins.then_inc(sem("peb_mm"), 1)
                te.wait_ge(sem("peb_ready"), 1)

            def compress(s):
                last = s == 3
                te.wait_ge(sem("cmp_in_sp"), 16 * (5 * PAGES - LATE if last else PAGES * (s + 1)))
                te.wait_ge(sem("cmp_in_po"), 16 * (3 * PAGES + LATE if last else PAGES * (s + 1)))
                if s >= 1:
                    te.wait_ge(sem("hc_ready"), 2 * s)
                raw = ring[:, 2:4, :].rearrange("p s n -> p (s n)").rearrange(
                    "p (j c l n) -> p c l j n", j=2 * PAGES, c=2, l=32)
                for c in range(2):
                    for l in range(32):
                        ins = mm(pb[6 + c][:, 0:128], w1[:, c, l, :], raw[:, c, l, :, :], l == 0, l == 31)
                    ins.then_inc(sem("cmp_mm"), 1)

            def compress_last():
                te.wait_ge(sem("hc_ready"), 8)
                hcv = hc.rearrange("p c (j g n) -> p c j g n", g=G, n=2)
                for g in range(G):
                    mm(pb[6][64 * g:64 * g + 64, 0:256], w2[:, 0, :], hcv[:, 0, :, g, :])
                for b in range(NB):
                    for g in range(G):
                        r = 32 * (b // HALF)
                        ins = mm(pb[7][r:r + 32, 128 * (b % HALF) + 64 * g:128 * (b % HALF) + 64 * g + 64],
                                 hc[:, 1, 64 * b + 32 * g:64 * b + 32 * g + 32], w2[:, 1, :])
                ins.then_inc(sem("comp_mm"), 1)

            turn = {BLK_Q: 4, BLK_KC: 3, BLK_KW: 1}

            def project(n):
                nb, i = divmod(n, TILES)
                a, b = CUT[nb]
                if i == 0:
                    te.wait_ge(sem("win_in%d" % (nb % 2)), 16 * (nb // 2 + 1))
                if n >= 4:
                    te.wait_ge(sem("proj_out"), n - 3)
                wv = ring[:, WIN_SLOT[nb], 0:KD * (b - a)].rearrange("p (k n) -> p k n", k=KD)
                for k in range(KD):
                    ins = mm(pb[n % 4][0:ROWS[i], 0:b - a], xT[:, k, i * P:i * P + ROWS[i]], wv[:, k, :],
                             k == 0, k == KD - 1)
                ins.then_inc(sem("proj_done"), 1)

            def turned(n):
                nb, i = divmod(n, TILES)
                rows = ROWS[i]
                t = n - BLK_Q * TILES
                te.wait_ge(sem("proj_out"), n + 1)
                if t >= 2:
                    te.wait_ge(sem("turn_out"), t - 1)
                if t == 11:
                    te.wait_ge(sem("pcmp_h"), 2)
                bank = pb[4 + t % 2]
                for m in range(turn[nb]):
                    if nb == BLK_Q:
                        src = stg[0:rows, n % 2, 128 * m:128 * m + 128]
                    elif nb == BLK_KC:
                        src = stk[0:rows, i % 4, 128 * m:128 * m + 128] if m < 2 else kvn[0:rows, i, 0:128]
                    else:
                        src = kvn[0:rows, i, 256:384]
                    ins = nc.tensor.transpose(bank[:, 128 * m:128 * m + rows], src, ident[0:rows, 0:rows])
                ins.then_inc(sem("turned"), 1)

            def block_of(nb):
                for n in range(nb * TILES, (nb + 1) * TILES):
                    project(n)
                    if nb >= BLK_Q and n % TILES:
                        turned(n - 1)
                if nb >= BLK_Q:
                    turned(n)

            te.wait_ge(sem("xn_ready"), KD)
            block_of(BLK_V)
            position_bias()
            compress(0)
            block_of(BLK_U)
            compress(1)
            block_of(BLK_Q)
            te.wait_ge(sem("proj_out"), 3 * TILES)
            te.wait_ge(sem("turn_out"), TILES)
            te.wait_ge(sem("vn_ready"), 1)
            te.wait_ge(sem("ws_ready"), 2)
            for g in range(GM):
                mm(pb[g // 2][:, 256 * (g % 2):256 * (g % 2) + 256], wst[:, g, :], vn[:, 0:PT, 64 * g:64 * g + 64])
                ins = mm(pb[4][0:NS, 64 * g:64 * g + 64], wss[:, g, :], vn[0:NS, PT, 64 * g:64 * g + 64])
            ins.then_inc(sem("gm_mm"), 1)
            compress(2)
            te.wait_ge(sem("gm_done"), 1)
            block_of(BLK_KC)
            compress(3)
            te.wait_ge(sem("turn_out"), 2 * TILES)
            for c in range(2):
                for l in range(32):
                    ins = mm(pb[5][:, 16 * c:16 * c + 16], w1[:, c, l, :], xp[:, c, l, :], l == 0, l == 31)
            ins.then_inc(sem("pcmp_mm"), 1)
            block_of(BLK_KW)
            compress_last()
            te.wait_ge(sem("turn_out"), 3 * TILES)
            te.wait_ge(sem("hrep_ready"), 1)
            for g in range(G):
                mm(pb[4][64 * g:64 * g + 64, 0:PBLK], w2[:, 0, :], hp[:, 0, PBLK * g:PBLK * (g + 1)])
            ins = mm(pb[4][0:64, 64:128], hrep, w2[:, 1, :])
            ins.then_inc(sem("pcomp_mm"), 1)

            def sampled(hf):
                te.wait_ge(sem("qbd_ready"), 1)
                te.wait_ge(sem("gate_ready"), 1)
                if hf == 0:
                    te.wait_ge(sem("proj_out"), 5 * TILES)
                    te.wait_ge(sem("pcomp_ready"), 2)
                    te.wait_ge(sem("comp_ready"), 2)
                else:
                    te.wait_ge(sem("combined"), 4)
                    te.wait_ge(sem("pcv_ready"), 2)
                mm(pb[7][:, 0:24], cst[0:32, C_SG + hf * P:C_SG + (hf + 1) * P], gates[0:32, PT, :])
                for q in range(HALF):
                    b = hf * HALF + q
                    r = slice(32 * q, 32 * q + 32)
                    ins = mm(pb[5][r, 0:32], qbd[:, b, :], kcs[:, 32 * b:32 * b + 32])
                    mm(pb[5][r, 64:96], qbd[:, b, :], kwT[:, SEQ:TOK])
                    ins = mm(pb[5][r, 96:128], qbd[:, b, :], ksT[:, SEQ:TOK])
                ins.then_inc(sem("samp_scores"), 1)
                te.wait_ge(sem("wst_in%d" % hf), 16)
                for q in range(HALF):
                    ins = mm(pb[4][32 * q:32 * q + 32, :], qbd[:, hf * HALF + q, :], ring[:, hf, 1024 * q:1024 * q + 512])
                ins.then_inc(sem("samp_scores"), 1)
                for q in range(HALF):
                    slot = SEL_SLOT[q]
                    te.wait_ge(sem("sel_in%d" % q), 16 * PAGES * (hf + 1))
                    kt = ring[:, slot, :].rearrange("p (j n) -> p j n", j=PAGES)
                    for m in range(4):
                        ins = mm(pb[m][32 * q:32 * q + 32, :], qbd[:, hf * HALF + q, :], kt[:, 4 * m:4 * m + 4, 0:128])
                ins.then_inc(sem("samp_scores"), 1)
                te.wait_ge(sem("pc_norm"), hf + 1)
                mm(pb[7][:, 32:64], cst[:, C_HS:C_HS + P], small[:, 96:128]).then_inc(sem("imp_mm"), 1)
                nc.tensor.transpose(pb[6][0:32, 0:128], small[:, 96:128], ident)
                te.wait_ge(sem("pw_ready"), hf + 1)
                for m in range(4):
                    nc.tensor.transpose(pb[4][:, 128 * m:128 * m + 128], pwin[:, 128 * m:128 * m + 128], ident)
                nc.tensor.transpose(pb[6][0:32, 128:256], pwin[:, WIN:WINW], ident).then_inc(sem("samp_tw"), 1)
                te.wait_ge(sem("ps_ready"), hf + 1)
                for m in range(PAGES):
                    ins = nc.tensor.transpose(pb[m // 4][:, 128 * (m % 4):128 * (m % 4) + 128],
                                              psel[:, 128 * m:128 * m + 128], ident)
                    if m % 4 == 3:
                        ins.then_inc(sem("samp_ts"), 1)
                nc.tensor.transpose(pb[7][0:32, 384:512], psel[:, PAST:SELW], ident).then_inc(sem("samp_ts"), 1)
                te.wait_ge(sem("samp_pt0"), 2 * hf + 2)
                for q in range(HALF):
                    b = hf * HALF + q
                    r = slice(32 * q, 32 * q + 32)
                    mm(pb[5][r, 0:128], ptc[hf][:, r], vcs(b))
                    for m in range(4):
                        mm(pb[6][r, 256:384], ptwin[:, m, r], ring[:, hf, 1024 * q + 512 + 128 * m:1024 * q + 640 + 128 * m],
                           m == 0, False)
                    mm(pb[6][r, 256:384], ptcw[:, r], kvn[0:32, PT, 384:512], False, True)
                te.wait_ge(sem("samp_pts"), 5 * hf + 5)
                for q in range(HALF):
                    slot = SEL_SLOT[q]
                    r = slice(32 * q, 32 * q + 32)
                    for m in range(PAGES):
                        mm(pb[6][r, 128:256], ptsel[:, m, r], ring[:, slot, 256 * m + 128:256 * m + 256], m == 0, False)
                    ins = mm(pb[6][r, 128:256], ptcs[:, r], kvn[0:32, PT, 128:256], False, True)
                ins.then_inc(sem("samp_pv"), 1)

            def prompt_compressed(i):
                if i >= 1:
                    te.wait_ge(sem("pcv_ready"), i)
                for hh in range(H):
                    r, h = gsel(hh)
                    bank = (pb[4], pb[7])[hh // HPG]
                    ins = mm(bank[:, 8 * hh:8 * hh + 8], qT[r, h, i * P:i * P + P], kcp[r, :])
                ins.then_inc(sem("pcs_mm"), 1)
                te.wait_ge(sem("pcp_ready"), i + 1)
                nc.tensor.transpose(pb[7][0:64, 0:128], small[:, 0:64], ident).then_inc(sem("pct_mm"), 1)
                te.wait_ge(sem("pct_out"), i + 1)
                mm(pb[4][:, :], pcT, vcp[:, :]).then_inc(sem("pcv_mm"), 1)

            def scores(u):
                i, b, hh = units[u]
                n = P * (i + 1)
                r, h = gsel(hh)
                if u >= 2:
                    te.wait_ge(sem("biased"), u - 1)
                kt = (ksT, kwT)[b]
                mm(pb[u % 2][:, 0:n], qT[r, h, i * P:i * P + P], kt[r, 0:n]).then_inc(sem("score_mm"), 1)

            def turn_probs(u):
                i = units[u][0]
                te.wait_ge(sem("probs"), u + 1)
                if u >= 2:
                    te.wait_ge(sem("pt_out"), u - 1)
                for m in range(i + 1):
                    ins = nc.tensor.transpose(pb[2 + u % 2][:, P * m:P * m + P], sb3[u % 3][:, P * m:P * m + P], ident)
                ins.then_inc(sem("pt_mm"), 1)

            def values(u):
                i, b, hh = units[u]
                te.wait_ge(sem("pt_out"), u + 1)
                pair = u // H
                if hh == 0 and pair >= 2:
                    te.wait_ge(sem("combined"), pair - 1)
                col = 128 + 256 * b + 64 * (hh // HPG)
                for m in range(i + 1):
                    ins = mm(pb[5 + b][:, 64 * hh:64 * hh + 64], pts[u % 2][:, P * m:P * m + P],
                             kvn[:, m, col:col + 64], m == 0, m == i)
                ins.then_inc(sem("pv_mm"), 1)

            def prompt(chunk):
                end = chunk[-1]
                for v in range(chunk[0], end + 3):
                    if v <= end and v % 16 == 0:
                        prompt_compressed(v // 16)
                    if v <= end:
                        scores(v)
                    if chunk[0] <= v - 1 <= end:
                        turn_probs(v - 1)
                    if chunk[0] <= v - 2 <= end:
                        values(v - 2)

            sampled(0)
            te.wait_ge(sem("samp_o"), 1)
            prompt(CHUNKS[0])
            sampled(1)
            te.wait_ge(sem("samp_o"), 2)
            prompt(CHUNKS[1])
            te.wait_ge(sem("combined"), 8)
            te.wait_ge(sem("samp_o"), 2)
            for hh in range(H):
                for hf in range(2):
                    at = C_SO + (hf * H + hh) * NS
                    ins = mm(pb[0][0:NS, 64 * hh:64 * hh + 64], cst[:, at:at + NS], osm[:, hf, :], hf == 0, hf == 1)
            ins.then_inc(sem("osamp_mm"), 1)

            def mix_turn(i):
                te.wait_ge(sem("mix_ready"), i + 1)
                if i >= 2:
                    te.wait_ge(sem("mixT_ready"), 8 * (i - 1))
                rows = ROWS[i]
                for k in range(KD):
                    src = (ov, ug)[k // 4][0:rows, i, P * (k % 4):P * (k % 4) + P]
                    ins = nc.tensor.transpose(pb[2 * (i % 2) + k // 4][:, P * (k % 4):P * (k % 4) + rows], src,
                                              ident[0:rows, 0:rows])
                ins.then_inc(sem("mix_used"), 1)

            wo = ring[:, 0:2, :].rearrange("p s n -> p (s n)").rearrange("p (k n) -> p k n", k=KD)

            def out_product(i):
                te.wait_ge(sem("mixT_ready"), 8 * (i + 1))
                te.wait_ge(sem("wout_in"), 16)
                for n in range(2):
                    if i >= 2:
                        te.wait_ge(sem("x2_ready"), 2 * (i - 2) + n + 1)
                    for k in range(KD):
                        ins = mm(pb[4 + 2 * (i % 2) + n][0:ROWS[i], :], mixT[i % 2][:, k, 0:ROWS[i]],
                                 wo[:, k, W * n:W * n + W], k == 0, k == KD - 1)
                    ins.then_inc(sem("out_mm"), 1)

            for i in range(TILES + 1):
                if i < TILES:
                    mix_turn(i)
                if i >= 1:
                    out_product(i - 1)

            te.wait_ge(sem("router_in"), 48)
            te.wait_ge(sem("x2_ready"), 2 * TILES)
            for i in range(TILES):
                rows = ROWS[i]
                te.wait_ge(sem("h2_ready"), i + 1)
                if i >= 1:
                    te.wait_ge(sem("h2T_ready"), 2 * i)
                for k in range(KD):
                    ins = nc.tensor.transpose(pb[k // 4][:, P * (k % 4):P * (k % 4) + rows],
                                              h2[i % 2][0:rows, P * k:P * k + P], ident[0:rows, 0:rows])
                ins.then_inc(sem("h2_turned"), 1)
                te.wait_ge(sem("h2T_ready"), 2 * (i + 1))
                if i >= 2:
                    te.wait_ge(sem("logit_out"), i - 1)
                for k in range(KD):
                    ins = mm(pb[4 + i % 2][0:rows, 0:20], h2T[:, k, 0:rows], wr[:, k, :], k == 0, k == KD - 1)
                ins.then_inc(sem("logit_mm"), 1)
            te.wait_ge(sem("onehot_ready"), 1)
            oh = rt[:, 0:TILES * E].rearrange("p (i e) -> p i e", e=E)
            for i in range(TILES):
                for j in range(i):
                    mm(pb[6][:, E * i:E * i + E], ones, oh[:, j, :], j == 0, False)
                mm(pb[6][:, E * i:E * i + E], cst[:, C_TRI:C_TRI + P], oh[:, i, :], i == 0, True)
            for j in range(TILES):
                ins = mm(pb[7][:, 0:E], ones, oh[:, j, :], j == 0, j == TILES - 1)
            ins.then_inc(sem("pos_mm"), 1)

            def gate_up(e, n, par, turn):
                te.wait_ge(sem("xe_in%d" % par), 16 * (turn + 1))
                after(te, "xt_ready", 2 * n)
                for k in range(KD):
                    ins = nc.tensor.transpose(pb[k // 4][:, P * (k % 4):P * (k % 4) + CAP],
                                              xe[par][0:CAP, P * k:P * k + P], ident[0:CAP, 0:CAP])
                ins.then_inc(sem("xt_mm"), 1)
                te.wait_ge(sem("xt_ready"), 2 * n + 2)
                after(te, "h_ready", n)
                for slots, bank, weights, done in ((WG, 2, "wg_in", "g_mm"), (WU, 3, "wu_in", "u_mm")):
                    te.wait_ge(sem(weights + "%d" % par), 16 * (turn + 1))
                    wv = ring[:, slots[par], :].rearrange("p (k f) -> p k f", k=KD)
                    for f in range(FE):
                        for k in range(KD):
                            ins = mm(pb[bank][:, CAP * f:CAP * f + CAP], wv[:, k, P * f:P * f + P],
                                     xeT[par][:, k, 0:CAP], k == 0, k == KD - 1)
                    ins.then_inc(sem(done), 1)

            def down(e, n, par, turn):
                te.wait_ge(sem("h_ready"), n + 1)
                te.wait_ge(sem("wd_in%d" % par), 16 * (turn + 1))
                after(te, "y_out", 2 * n)
                wv = ring[:, WD[par], :].rearrange("p (f n) -> p f n", f=FE)
                for c in range(2):
                    for f in range(FE):
                        ins = mm(pb[4 + c][0:CAP, :], he[par][:, f, 0:CAP], wv[:, f, W * c:W * c + W], f == 0, f == FE - 1)
                    ins.then_inc(sem("y_mm"), 1)

            expert_units(0, gate_up, te, down)
            te.wait_ge(sem("flag_ready"), 1)
            more = te.value_load(ints[0:1, 80:81], min_val=0, max_val=1)
            with te.If(more != 0):
                with te.Fori(1, PASSES) as b:
                    expert_units(b, gate_up, te, down)

        @block.scalar
        def _(act):
            A = nc.scalar.activation
            act.wait_ge(sem("x_in"), 16)
            for k in range(KD):
                A(sq[k], xT[:, k, :], ACT.Square).then_inc(sem("sq_ready"), 1)
            act.wait_ge(sem("recip"), 1)
            A(rb, rb, ACT.Sqrt).then_inc(sem("rstd"), 1)

            def compress(s):
                for c in range(2):
                    act.wait_ge(sem("cmp_mm"), 2 * s + c + 1)
                    bank = pb[6 + c]
                    if c == 0:
                        A(hc[:, c, P * s:P * s + P], bank[:, 0:128], ACT.Gelu_apprx_tanh,
                          bias=peb[:, c:c + 1]).then_inc(sem("hc_ready"), 1)
                        continue
                    for b in range(2):
                        at = P * s + 64 * b
                        ins = A(hc[:, c, at:at + 64].rearrange("p (g j n) -> p j g n", g=G, n=2),
                                bank[:, 64 * b:64 * b + 64].rearrange("p (j g n) -> p j g n", g=G, n=2),
                                ACT.Gelu_apprx_tanh, bias=peb[:, c:c + 1])
                    ins.then_inc(sem("hc_ready"), 1)

            def projected(n):
                nb, i = divmod(n, TILES)
                rows = ROWS[i]
                act.wait_ge(sem("proj_done"), n + 1)
                bank = pb[n % 4]
                if nb <= BLK_U:
                    A((vn, ug)[nb][0:rows, i, :], bank[0:rows, :], ACT.Gelu_apprx_tanh).then_inc(sem("proj_out"), 1)
                elif nb == BLK_Q:
                    if i >= 2:
                        act.wait_ge(sem("turned"), i - 1)
                    nc.scalar.mul(stg[0:rows, n % 2, :].rearrange("p (h g d) -> p g h d", h=HPG, g=G),
                                  bank[0:rows, :].rearrange("p (g h d) -> p g h d", h=HPG, g=G), -(HD ** -0.5)).then_inc(sem("proj_out"), 1)
                elif nb == BLK_KC:
                    if i == 0:
                        act.wait_ge(sem("turned"), TILES)
                    elif i == 4:
                        act.wait_ge(sem("turned"), TILES + 1)
                        act.wait_ge(sem("kvc_first"), 16)
                    nc.scalar.copy(stk[0:rows, i % 4, :], bank[0:rows, 0:256])
                    nc.scalar.copy(kvn[0:rows, i, 0:256], bank[0:rows, 256:512]).then_inc(sem("proj_out"), 1)
                else:
                    nc.scalar.copy(kvn[0:rows, i, 256:512], bank[0:rows, 0:256])
                    nc.scalar.copy(gates[0:rows, i, :], bank[0:rows, 256:280]).then_inc(sem("proj_out"), 1)

            def block_of(nb):
                for n in range(nb * TILES, (nb + 1) * TILES):
                    projected(n)

            act.wait_ge(sem("ss_mm"), 1)
            block_of(BLK_V)
            act.wait_ge(sem("peb_mm"), 1)
            nc.scalar.copy(peb[:, :], pb[7][:, 0:2]).then_inc(sem("peb_ready"), 1)
            act.wait_ge(sem("peb_ready"), 1)
            compress(0)
            block_of(BLK_U)
            compress(1)
            act.wait_ge(sem("recip"), 2)
            A(lst, lst, ACT.Sqrt).then_inc(sem("rstd"), 1)
            act.wait_ge(sem("xn_ready"), KD)
            block_of(BLK_Q)
            compress(2)
            block_of(BLK_KC)
            compress(3)
            act.wait_ge(sem("pcmp_mm"), 1)
            for c in range(2):
                A(hp[:, c, :], pb[5][:, 16 * c:16 * c + 16], ACT.Gelu_apprx_tanh,
                  bias=peb[:, c:c + 1]).then_inc(sem("pcmp_h"), 1)
            act.wait_ge(sem("gates_zero"), 1)
            block_of(BLK_KW)
            act.wait_ge(sem("proj_out"), 5 * TILES)
            A(gates[:, :, :], gates[:, :, :], ACT.Exp, scale=-1.0).then_inc(sem("gate_exp"), 1)
            act.wait_ge(sem("comp_mm"), 1)
            for n in range(2):
                ins = nc.scalar.copy(kvn[32 + 32 * n:64 + 32 * n, PT, :], pb[7][32 * n:32 * n + 32, :])
            ins.then_inc(sem("comp_ready"), 1)

            def sampled(hf):
                act.wait_ge(sem("samp_biased"), 3 * hf + 1)
                A(small[:, 96:128], small[:, 96:128], ACT.Exp, scale=-1.0, bias=small[:, 128:129],
                  accum_out=small[:, 131:132]).then_inc(sem("pc_exp"), 1)
                act.wait_ge(sem("samp_biased"), 3 * hf + 2)
                A(pwin, pwin, ACT.Exp, scale=-1.0, bias=small[:, 130:131],
                  accum_out=small[:, 133:134]).then_inc(sem("pw_ready"), 1)
                act.wait_ge(sem("samp_tw"), hf + 1)
                nc.scalar.copy(ptc[hf], pb[6][0:32, 0:128])
                nc.scalar.copy(ptwin.rearrange("p c n -> p (c n)"), pb[4][:, :]).then_inc(sem("samp_pt0"), 1)
                nc.scalar.copy(ptcw, pb[6][0:32, 128:256]).then_inc(sem("samp_pt0"), 1)
                act.wait_ge(sem("samp_biased"), 3 * hf + 3)
                A(psel, psel, ACT.Exp, scale=-1.0, bias=small[:, 129:130],
                  accum_out=small[:, 132:133]).then_inc(sem("ps_ready"), 1)

            def prompt(chunk):
                for u in chunk:
                    i, b, hh = units[u]
                    n = P * (i + 1)
                    if u % 16 == 0:
                        act.wait_ge(sem("pcx_ready"), i + 1)
                        A(small[:, 0:64], small[:, 0:64], ACT.Exp, scale=-1.0).then_inc(sem("pce_ready"), 1)
                        act.wait_ge(sem("pcv_mm"), i + 1)
                        nc.scalar.copy(ov[:, i, :], pb[4][:, :]).then_inc(sem("pcv_ready"), 1)
                    if hh == 0 and u >= 16:
                        act.wait_ge(sem("combined"), u // H - 1)
                    act.wait_ge(sem("biased"), u + 1)
                    A(sb3[u % 3][:, 0:n], sb3[u % 3][:, 0:n], ACT.Exp, scale=-1.0, bias=rt[:, 128 + u % 4:129 + u % 4],
                      accum_out=rt[:, 136 + 8 * (u // H % 2) + hh:137 + 8 * (u // H % 2) + hh]).then_inc(sem("probs"), 1)

            sampled(0)
            prompt(CHUNKS[0])
            sampled(1)
            prompt(CHUNKS[1])
            act.wait_ge(sem("osamp_mm"), 1)
            nc.scalar.copy(ov[0:NS, PT, :], pb[0][0:NS, :]).then_inc(sem("osamp_out"), 1)
            act.wait_ge(sem("osamp_out"), 1)
            act.wait_ge(sem("attn_done"), 1)
            for i in range(TILES):
                for m in range(2):
                    A(work[0:ROWS[i], 2560:3072], (ov, ug)[m][0:ROWS[i], i, :], ACT.Square,
                      accum_out=small[0:ROWS[i], 2 * i + m:2 * i + m + 1]).then_inc(sem("mix_sq"), 1)
                    act.wait_ge(sem("mix_sq"), 2 * i + m + 1)
            act.wait_ge(sem("recip"), 3)
            A(small[:, 0:10], small[:, 0:10], ACT.Sqrt).then_inc(sem("rstd"), 1)
            for i in range(TILES):
                act.wait_ge(sem("mix_used"), i + 1)
                if i >= 2:
                    act.wait_ge(sem("out_mm"), 2 * (i - 1))
                for k in range(KD):
                    A(mixT[i % 2][:, k, 0:ROWS[i]], pb[2 * (i % 2) + k // 4][:, P * (k % 4):P * (k % 4) + ROWS[i]],
                      ACT.Copy, scale=vec[:, KD + k:KD + k + 1]).then_inc(sem("mixT_ready"), 1)
            for i in range(TILES):
                act.wait_ge(sem("x2_ready"), 2 * (i + 1))
                if i == 0:
                    act.wait_ge(sem("out_mm"), 2 * TILES)
                else:
                    act.wait_ge(sem("x2_sq"), i)
                A(work[0:ROWS[i], 0:1024], x2[0:ROWS[i], i, :], ACT.Square,
                  accum_out=small[0:ROWS[i], 16 + i:17 + i]).then_inc(sem("x2_sq"), 1)
            act.wait_ge(sem("recip"), 4)
            A(small[:, 16:21], small[:, 16:21], ACT.Sqrt).then_inc(sem("rstd"), 1)
            for i in range(TILES):
                act.wait_ge(sem("h2_turned"), i + 1)
                if i >= 1:
                    act.wait_ge(sem("logit_mm"), i)
                nc.scalar.copy(h2T[:, 0:4, 0:ROWS[i]],
                               pb[0][:, :].rearrange("p (k n) -> p k n", k=4)[:, :, 0:ROWS[i]]).then_inc(sem("h2T_ready"), 1)
            act.wait_ge(sem("rt_shifted"), 1)
            A(rt[:, 220:240], rt[:, 220:240], ACT.Exp).then_inc(sem("rt_exp"), 1)
            act.wait_ge(sem("rt_shifted"), 2)
            A(rt[:, 260:265], rt[:, 260:265], ACT.Exp).then_inc(sem("rt_exp"), 1)

            def turn_silu(e, n, par, turn):
                act.wait_ge(sem("xt_mm"), n + 1)
                after(act, "u_mm", n - 1)
                nc.scalar.copy(xeT[par][:, 0:4, 0:CAP], pb[0][:, :].rearrange("p (k n) -> p k n", k=4)[:, :, 0:CAP]
                               ).then_inc(sem("xt_ready"), 1)
                act.wait_ge(sem("g_mm"), n + 1)
                after(act, "h_ready", n - 1)
                A(sg[par][:, :, 0:CAP], pb[2][:, 0:FE * CAP].rearrange("p (f n) -> p f n", f=FE), ACT.Silu).then_inc(sem("silu"), 1)

            def y_out(e, n, par, turn):
                act.wait_ge(sem("y_mm"), 2 * n + 1)
                after(act, "y_stored%d" % par, 16 * turn)
                nc.scalar.copy(ye[par][0:CAP, 0:512], pb[4][0:CAP, :]).then_inc(sem("y_out"), 1)

            expert_units(0, turn_silu, act, y_out)
            act.wait_ge(sem("flag_ready"), 1)
            more = act.value_load(ints[0:1, 80:81], min_val=0, max_val=1)
            with act.If(more != 0):
                with act.Fori(1, PASSES) as b:
                    expert_units(b, turn_silu, act, y_out)
            for i in range(TILES):
                act.wait_ge(sem("x3_ready"), i + 1)
                A(yg[2 * i + 1][0:ROWS[i], :], x2[0:ROWS[i], i, :], ACT.Square,
                  accum_out=small[0:ROWS[i], 32 + i:33 + i]).then_inc(sem("x3_sq"), 1)
            act.wait_ge(sem("recip"), 5)
            A(small[:, 32:37], small[:, 32:37], ACT.Sqrt).then_inc(sem("rstd"), 1)

        @block.vector
        def _(dve):
            V = nc.vector
            chain = [0]

            def link(ins):
                chain[0] += 1
                ins.then_inc(sem("dve_step"), 1)
                dve.wait_ge(sem("dve_step"), chain[0])

            V.memset(gates[:, :, :], 0.0).then_inc(sem("gates_zero"), 1)
            link(V.memset(qbd[:, :, :], 0.0))
            link(V.memset(rt[:, :], 0.0))
            link(V.memset(small[:, :], 1.0))
            dve.wait_ge(sem("ss_mm"), 1)
            for n in range(2):
                link(V.tensor_scalar(rb[:, 272 * n:272 * n + 272], pb[4 + n][:, 0:272], 1.0 / D, EPS, ALU.mult, ALU.add))
            V.reciprocal(rb, rb).then_inc(sem("recip"), 1)
            dve.wait_ge(sem("rstd"), 1)
            dve.wait_ge(sem("pe_in"), 64)
            for k in range(KD):
                V.scalar_tensor_tensor(out=xT[:, k, :], in0=xT[:, k, :], scalar=vec[:, k:k + 1], in1=rb,
                                       op0=ALU.mult, op1=ALU.mult).then_inc(sem("xn_ready"), 1)
            def turned(t):
                nb, i = divmod(t + BLK_Q * TILES, TILES)
                rows = ROWS[i]
                dve.wait_ge(sem("turned"), t + 1)
                bank = pb[4 + t % 2]
                if nb == BLK_Q:
                    ins = V.tensor_copy(qT[:, :, i * P:i * P + rows],
                                        bank[:, :].rearrange("p (h n) -> p h n", h=HPG)[:, :, 0:rows])
                elif nb == BLK_KC:
                    if i < PT:
                        for c in range(2):
                            src = bank[:, 128 * c:128 * c + 128].rearrange("p (b l q) -> p q l b", b=2, q=2)
                            for g in range(G):
                                for q in range(2):
                                    V.tensor_copy(xp[64 * q:64 * q + 64, c, :, PBLK * g + 2 * i:PBLK * g + 2 * i + 2],
                                                  src[64 * g:64 * g + 64, q, :, :])
                    ins = V.tensor_copy(ksT[:, i * P:i * P + rows], bank[:, 256:256 + rows])
                else:
                    ins = V.tensor_copy(kwT[:, i * P:i * P + rows], bank[:, 128 * 0:rows])
                ins.then_inc(sem("turn_out"), 1)
                if t == TILES - 1:
                    dve.wait_ge(sem("turn_out"), TILES)
                    for g in range(G):
                        ins = V.tensor_copy(
                            qbd[64 * g:64 * g + 64, :, 16 * g:16 * g + 16].rearrange("p b (h n) -> p b h n", h=HPG),
                            qT[64 * g:64 * g + 64, :, SEQ:TOK].rearrange("p h (b n) -> p b h n", b=NB))
                        ins.then_inc(sem("qbd_part"), 1)
                    dve.wait_ge(sem("qbd_part"), 2)
                    dve.sem_inc(sem("qbd_ready"), 1)

            dve.wait_ge(sem("gm_in"), 96)
            dve.wait_ge(sem("cst_in"), 16)
            link(V.memset(lst, 1.0))
            for i in range(TILES):
                rows = ROWS[i]
                dve.wait_ge(sem("proj_out"), i + 1)
                v = vn[0:rows, i, :].rearrange("p (g d) -> p g d", g=GM)
                mean, var = small[0:rows, 136:144], lst[0:rows, 8 * i:8 * i + 8]
                link(V.tensor_reduce(mean, v, AX, ALU.add))
                link(V.tensor_scalar(mean, mean, 1.0 / HD, None, ALU.mult))
                link(V.tensor_tensor(v, v, mean[:, :, None].to_broadcast([rows, GM, HD]), ALU.subtract))
                s2 = lsq[0:rows, :].rearrange("p (g d) -> p g d", g=GM)
                link(V.tensor_tensor(s2, v, v, ALU.mult))
                link(V.tensor_reduce(var, s2, AX, ALU.add))
            link(V.tensor_scalar(lst, lst, 1.0 / HD, EPS, ALU.mult, ALU.add))
            V.reciprocal(lst, lst).then_inc(sem("recip"), 1)
            V.tensor_tensor(wst, wst, cst[:, C_TRI:C_TRI + P][:, None, :].to_broadcast([P, GM, P]), ALU.mult
                            ).then_inc(sem("ws_ready"), 1)
            V.tensor_tensor(wss, wss, cst[0:NS, C_WS:C_WS + NS][:, None, :].to_broadcast([NS, GM, NS]), ALU.mult
                            ).then_inc(sem("ws_ready"), 1)
            dve.wait_ge(sem("rstd"), 2)
            for i in range(TILES):
                rows = ROWS[i]
                v = vn[0:rows, i, :].rearrange("p (g d) -> p g d", g=GM)
                r = lst[0:rows, 8 * i:8 * i + 8]
                link(V.tensor_tensor(v, v, r[:, :, None].to_broadcast([rows, GM, HD]), ALU.mult))
                link(V.tensor_tensor(vn[0:rows, i, :], vn[0:rows, i, :], lng[0:rows, :], ALU.mult))
                link(V.tensor_tensor(vn[0:rows, i, :], vn[0:rows, i, :], lnb[0:rows, :], ALU.add))
            dve.sem_inc(sem("vn_ready"), 1)
            for t in range(TILES):
                turned(t)
            dve.wait_ge(sem("gm_mm"), 1)
            dve.wait_ge(sem("proj_out"), 2 * TILES)
            for g in range(GM):
                u = ug[:, 0:PT, 64 * g:64 * g + 64]
                src = pb[g // 2][:, 256 * (g % 2):256 * (g % 2) + 256].rearrange("p (c d) -> p c d", c=PT)
                V.scalar_tensor_tensor(out=u, in0=src, scalar=bst[:, g:g + 1], in1=u, op0=ALU.add, op1=ALU.mult)
                u = ug[0:NS, PT, 64 * g:64 * g + 64]
                ins = V.scalar_tensor_tensor(out=u, in0=pb[4][0:NS, 64 * g:64 * g + 64], scalar=bss[:, g:g + 1], in1=u,
                                             op0=ALU.add, op1=ALU.mult)
            link(ins)
            dve.wait_ge(sem("gmv_out"), 16)
            dve.sem_inc(sem("gm_done"), 1)
            for t in range(TILES, 2 * TILES):
                turned(t)
            dve.wait_ge(sem("pcmp_h"), 2)
            V.tensor_copy(hrep.rearrange("p (g h n) -> p g h n", g=G, h=HPG),
                          hp[:, 1, :].rearrange("p (g n) -> p g n", g=G)[:, :, None, :].to_broadcast([P, G, HPG, PBLK])
                          ).then_inc(sem("hrep_ready"), 1)
            for t in range(2 * TILES, 3 * TILES):
                turned(t)
            dve.wait_ge(sem("gate_exp"), 1)
            gall = gates[:, :, :].rearrange("p i n -> p (i n)")
            link(V.tensor_scalar(gall, gall, 1.0, None, ALU.add))
            link(V.reciprocal(gall, gall))
            dve.sem_inc(sem("gate_ready"), 1)
            dve.wait_ge(sem("comp_mm"), 1)
            V.tensor_copy(kcs[:, :], pb[6][:, 0:256]).then_inc(sem("comp_ready"), 1)
            dve.wait_ge(sem("pcomp_mm"), 1)
            V.tensor_copy(kcp[:, :], pb[4][:, 0:PBLK]).then_inc(sem("pcomp_ready"), 1)
            link(V.tensor_copy(small[0:64, 96:160], pb[4][0:64, 64:128]))
            V.tensor_tensor(vcp[:, :].rearrange("p (h d) -> p h d", h=H),
                            small[0:64, 96:160][:, None, :].to_broadcast([64, H, HD]),
                            cst[0:64, C_VM:C_VM + H][:, :, None].to_broadcast([64, H, HD]), ALU.mult
                            ).then_inc(sem("pcomp_ready"), 1)
            dve.sem_inc(sem("earlier_free"), 1)

            mc, ms, mw = (small[:, 128 + k:129 + k] for k in range(3))
            lc, ls, lw = (small[:, 131 + k:132 + k] for k in range(3))
            m2 = small[:, 134:135]
            gr = small[:, 136:139]
            pc = small[:, 96:128]

            def ttr(out, a, b, acc):
                return V.tensor_tensor_reduce(out, a, b, 1.0, 3.0e38, ALU.add, ALU.min, acc)

            def sampled(hf):
                cur = small[:, 0:32]
                link(V.memset(cur, BIG))
                link(V.tensor_copy(cur[:, 16 * hf:16 * hf + 16], cst[:, C_CU:C_CU + 16]))
                dve.wait_ge(sem("samp_scores"), 3 * hf + 1)
                t24 = small[:, 32:56]
                link(V.tensor_tensor(t24, pb[7][:, 0:24], cst[:, C_HM:C_HM + 24], ALU.mult))
                link(V.tensor_reduce(gr, t24.rearrange("p (b h) -> p b h", b=3), AX, ALU.add))
                ttr(pc, pb[5][:, 0:32], cst[:, C_SB:C_SB + BLKS], mc).then_inc(sem("samp_biased"), 1)
                dve.wait_ge(sem("samp_scores"), 3 * hf + 2)
                link(ttr(pwin[:, 0:WIN], pb[4][:, :], cst[:, C_WB:C_WB + WIN], mw))
                link(ttr(pwin[:, WIN:WINW], pb[5][:, 64:96], cur, m2))
                V.tensor_tensor(mw, mw, m2, ALU.min).then_inc(sem("samp_biased"), 1)
                dve.wait_ge(sem("pc_exp"), hf + 1)
                link(V.reciprocal(lc, lc))
                V.tensor_scalar(pc, pc, lc, None, ALU.mult).then_inc(sem("pc_norm"), 1)
                imp = small[:, 56:88]
                dve.wait_ge(sem("imp_mm"), hf + 1)
                link(V.tensor_copy(imp, pb[7][:, 32:64]))
                other = imp[:, None, :].to_broadcast([P, BLKS, BLKS])
                own = imp[:, :, None].to_broadcast([P, BLKS, BLKS])
                r1, r2 = rt[:, 160:192], rt[:, 192:224]
                link(V.tensor_tensor(rank, other, own, ALU.is_gt))
                link(V.tensor_reduce(r1, rank, AX, ALU.add))
                link(V.tensor_tensor(rank, other, own, ALU.is_equal))
                dve.wait_ge(sem("earlier_in"), 16 * (hf + 1))
                link(V.tensor_tensor(rank, rank, earlier.rearrange("p (a b) -> p a b", a=BLKS), ALU.mult))
                link(V.tensor_reduce(r2, rank, AX, ALU.add))
                link(V.tensor_tensor(r1, r1, r2, ALU.add))
                link(V.tensor_scalar(r1, r1, NSEL - 0.5, BIG, ALU.is_gt, ALU.mult))
                link(V.tensor_tensor(r1, r1, cst[:, C_BL:C_BL + BLKS], ALU.add))
                dve.wait_ge(sem("samp_scores"), 3 * hf + 3)
                for m in range(4):
                    ins = V.tensor_tensor(psel[:, 512 * m:512 * m + 512].rearrange("p (b l) -> p b l", b=8),
                                          pb[m][:, :].rearrange("p (b l) -> p b l", b=8),
                                          r1[:, 8 * m:8 * m + 8][:, :, None].to_broadcast([P, 8, L]), ALU.add)
                link(ins)
                s3 = psel[:, 0:PAST].rearrange("p (b l) -> p b l", b=BLKS)
                link(V.tensor_tensor(s3, s3, cst[:, C_OF:C_OF + L][:, None, :].to_broadcast([P, BLKS, L]), ALU.add))
                link(ttr(psel[:, PAST:SELW], pb[5][:, 96:128], cur, m2))
                link(V.tensor_reduce(ms, psel[:, 0:PAST], AX, ALU.min))
                V.tensor_tensor(ms, ms, m2, ALU.min).then_inc(sem("samp_biased"), 1)
                for m in range(4):
                    dve.wait_ge(sem("samp_ts"), 5 * hf + m + 1)
                    V.tensor_copy(ptsel[:, 4 * m:4 * m + 4, :].rearrange("p c n -> p (c n)"), pb[m][:, :]
                                  ).then_inc(sem("samp_pts"), 1)
                dve.wait_ge(sem("samp_ts"), 5 * hf + 5)
                V.tensor_copy(ptcs, pb[7][0:32, 384:512]).then_inc(sem("samp_pts"), 1)
                dve.wait_ge(sem("ps_ready"), hf + 1)
                link(V.reciprocal(small[:, 132:134], small[:, 132:134]))
                link(V.tensor_tensor(gr[:, 1:3], gr[:, 1:3], small[:, 132:134], ALU.mult))
                dve.wait_ge(sem("samp_pv"), hf + 1)
                acc = rt[:, 224:352]
                link(V.tensor_scalar(acc, pb[5][:, 0:128], gr[:, 0:1], None, ALU.mult))
                for m in (1, 2):
                    link(V.scalar_tensor_tensor(out=acc, in0=pb[6][:, 128 * m:128 * m + 128], scalar=gr[:, m:m + 1],
                                                in1=acc, op0=ALU.mult, op1=ALU.add))
                link(V.tensor_scalar(osm[:, hf, :], acc[:, 0:64], cst[:, C_GM:C_GM + 1], None, ALU.mult))
                V.scalar_tensor_tensor(out=osm[:, hf, :], in0=acc[:, 64:128], scalar=cst[:, C_GM + 1:C_GM + 2],
                                       in1=osm[:, hf, :], op0=ALU.mult, op1=ALU.add).then_inc(sem("samp_o"), 1)
                dve.wait_ge(sem("samp_o"), hf + 1)

            def bias(u):
                i, b, hh = units[u]
                n = P * (i + 1)
                dve.wait_ge(sem("score_mm"), u + 1)
                if u >= 3:
                    dve.wait_ge(sem("pt_mm"), u - 2)
                ttr(sb3[u % 3][:, 0:n], pb[u % 2][:, 0:n], alibi[:, hh, SEQ - n:SEQ], rt[:, 128 + u % 4:129 + u % 4]
                    ).then_inc(sem("biased"), 1)

            def probs_out(u):
                n = P * (units[u][0] + 1)
                dve.wait_ge(sem("pt_mm"), u + 1)
                if u >= 2:
                    dve.wait_ge(sem("pv_mm"), u - 1)
                V.tensor_copy(pts[u % 2][:, 0:n], pb[2 + u % 2][:, 0:n]).then_inc(sem("pt_out"), 1)

            def compressed(i):
                x = small[:, 0:64]
                x3 = x.rearrange("p (h n) -> p h n", h=H)
                mx, sm = small[:, 64:72], small[:, 72:80]
                dve.wait_ge(sem("pcs_mm"), i + 1)
                for g in range(G):
                    at = C_PB + 64 * i + 32 * g
                    ins = V.tensor_tensor(x[:, 32 * g:32 * g + 32], (pb[4], pb[7])[g][:, 32 * g:32 * g + 32],
                                          cst[:, at:at + 32], ALU.add)
                link(ins)
                link(V.tensor_reduce(mx, x3, AX, ALU.min))
                V.tensor_tensor(x3, x3, mx[:, :, None].to_broadcast([P, H, PBLK]), ALU.subtract
                                ).then_inc(sem("pcx_ready"), 1)
                dve.wait_ge(sem("pce_ready"), i + 1)
                link(V.tensor_reduce(sm, x3, AX, ALU.add))
                link(V.reciprocal(sm, sm))
                link(V.tensor_tensor(sm, sm, gates[:, i, 0:8], ALU.mult))
                link(V.tensor_tensor(x, x, cst[:, C_PM + 64 * i:C_PM + 64 * i + 64], ALU.mult))
                V.tensor_tensor(x3, x3, sm[:, :, None].to_broadcast([P, H, PBLK]), ALU.mult
                                ).then_inc(sem("pcp_ready"), 1)
                dve.wait_ge(sem("pct_mm"), i + 1)
                if i >= 1:
                    dve.wait_ge(sem("pcv_mm"), i)
                V.tensor_copy(rt[0:64, 0:128], pb[7][0:64, 0:128]).then_inc(sem("pct_out"), 1)

            def combine(pair):
                i, b = divmod(pair, 2)
                dve.wait_ge(sem("pv_mm"), H * (pair + 1))
                dve.wait_ge(sem("probs"), H * (pair + 1))
                if b == 0:
                    dve.wait_ge(sem("pcv_ready"), i + 1)
                at = 136 + 8 * (pair % 2)
                ri = rt[:, 152:160]
                link(V.reciprocal(ri, rt[:, at:at + 8]))
                link(V.tensor_tensor(ri, ri, gates[:, i, 8 + 8 * b:16 + 8 * b], ALU.mult))
                link(V.tensor_tensor(branch.rearrange("p (h d) -> p h d", h=H),
                                     pb[5 + b][:, :].rearrange("p (h d) -> p h d", h=H),
                                     ri[:, :, None].to_broadcast([P, H, HD]), ALU.mult))
                V.tensor_tensor(ov[:, i, :], ov[:, i, :], branch, ALU.add).then_inc(sem("combined"), 1)
                dve.wait_ge(sem("combined"), pair + 1)

            def prompt(chunk):
                end = chunk[-1]
                for v in range(chunk[0], end + 3):
                    if v <= end and v % 16 == 0:
                        compressed(v // 16)
                    if v <= end:
                        bias(v)
                    if chunk[0] <= v - 1 <= end:
                        probs_out(v - 1)
                    if chunk[0] <= v - 2 <= end and (v - 2) % H == H - 1:
                        combine((v - 2) // H)

            sampled(0)
            dve.wait_ge(sem("alibi_in"), 16)
            prompt(CHUNKS[0])
            dve.sem_inc(sem("earlier_free"), 1)
            sampled(1)
            prompt(CHUNKS[1])
            link(V.memset(small[:, 0:48], 1.0))
            dve.sem_inc(sem("attn_done"), 1)

            dve.wait_ge(sem("mix_sq"), 2 * TILES)
            rs = small[:, 0:10]
            link(V.tensor_scalar(rs, rs, 1.0 / W, EPS, ALU.mult, ALU.add))
            V.reciprocal(rs, rs).then_inc(sem("recip"), 1)
            dve.wait_ge(sem("rstd"), 3)
            for i in range(TILES):
                rows = ROWS[i]
                for m in range(2):
                    v = (ov, ug)[m][0:rows, i, :]
                    ins = V.tensor_scalar(v, v, small[0:rows, 2 * i + m:2 * i + m + 1], None, ALU.mult)
                    if m == 0:
                        link(ins)
                ins.then_inc(sem("mix_ready"), 1)
            dve.wait_ge(sem("xnat_in"), 16 * TILES)
            for i in range(TILES):
                for n in range(2):
                    dve.wait_ge(sem("out_mm"), 2 * i + n + 1)
                    v = x2[0:ROWS[i], i, W * n:W * n + W]
                    V.tensor_tensor(v, pb[4 + 2 * (i % 2) + n][0:ROWS[i], :], v, ALU.add).then_inc(sem("x2_ready"), 1)
            dve.wait_ge(sem("x2_sq"), TILES)
            rs = small[:, 16:21]
            link(V.tensor_scalar(rs, rs, 1.0 / D, EPS, ALU.mult, ALU.add))
            V.reciprocal(rs, rs).then_inc(sem("recip"), 1)
            dve.wait_ge(sem("rstd"), 4)
            dve.wait_ge(sem("router_in"), 48)
            lg = rt[:, 80:180].rearrange("p (i n) -> p i n", i=TILES)
            link(V.memset(rt[:, 80:180], 0.0))
            for i in range(TILES + 1):
                if i < TILES:
                    rows = ROWS[i]
                    if i >= 2:
                        dve.wait_ge(sem("h2_turned"), i - 1)
                        dve.wait_ge(sem("h2_out%d" % (i % 2)), 16 * (i // 2))
                    V.scalar_tensor_tensor(out=h2[i % 2][0:rows, :], in0=x2[0:rows, i, :],
                                           scalar=small[0:rows, 16 + i:17 + i], in1=g2[0:rows, :],
                                           op0=ALU.mult, op1=ALU.mult).then_inc(sem("h2_ready"), 1)
                if i >= 1:
                    dve.wait_ge(sem("logit_mm"), i)
                    r1 = ROWS[i - 1]
                    V.tensor_tensor(lg[0:r1, i - 1, :], pb[4 + (i - 1) % 2][0:r1, 0:20], br[0:r1, :], ALU.add
                                    ).then_inc(sem("logit_out"), 1)
                if i < TILES:
                    dve.wait_ge(sem("h2_turned"), i + 1)
                    if i >= 1:
                        dve.wait_ge(sem("logit_mm"), i)
                    V.tensor_copy(h2T[:, 4:8, 0:rows],
                                  pb[1][:, :].rearrange("p (k n) -> p k n", k=4)[:, :, 0:rows]).then_inc(sem("h2T_ready"), 1)
            dve.wait_ge(sem("logit_out"), TILES)

            def b3(x, n):
                return x[:, :, None].to_broadcast([P, TILES, n])

            def col(a):
                return rt[:, a:a + TILES]

            def mat(a, n):
                return rt[:, a:a + TILES * n].rearrange("p (i n) -> p i n", n=n)

            i4 = cst[:, C_IE:C_IE + 4][:, None, :].to_broadcast([P, TILES, 4])
            i16 = cst[:, C_IE:C_IE + E][:, None, :].to_broadcast([P, TILES, E])

            def first_of(x, top, idx, tmp):
                link(V.tensor_tensor(tmp, x, b3(top, 4), ALU.not_equal))
                link(V.tensor_scalar(tmp, tmp, 16.0, None, ALU.mult))
                link(V.tensor_tensor(tmp, tmp, i4, ALU.add))
                link(V.tensor_reduce(idx, tmp, AX, ALU.min))

            lgg = lg[:, :, 0:4]
            gmax, grp, tmp4 = col(180), col(185), mat(190, 4)
            link(V.tensor_reduce(gmax, lgg, AX, ALU.max))
            first_of(lgg, gmax, grp, tmp4)
            ge = mat(220, 4)
            V.tensor_tensor(ge, lgg, b3(gmax, 4), ALU.subtract).then_inc(sem("rt_shifted"), 1)
            oh4, le = mat(240, 4), mat(265, 4)
            link(V.tensor_tensor(oh4, i4, b3(grp, 4), ALU.is_equal))
            link(V.memset(rt[:, 265:285], 0.0))
            for g in range(4):
                link(V.tensor_tensor(tmp4, lg[:, :, 4 + 4 * g:8 + 4 * g], oh4[:, :, g:g + 1].to_broadcast([P, TILES, 4]),
                                     ALU.mult))
                link(V.tensor_tensor(le, le, tmp4, ALU.add))
            top1, top2, id1, id2, w1c, w2c = (col(285 + 5 * k) for k in range(6))
            link(V.tensor_reduce(top1, le, AX, ALU.max))
            first_of(le, top1, id1, tmp4)
            link(V.tensor_tensor(tmp4, i4, b3(id1, 4), ALU.is_equal))
            link(V.tensor_scalar(tmp4, tmp4, -BIG, None, ALU.mult))
            link(V.tensor_tensor(le, le, tmp4, ALU.add))
            link(V.tensor_reduce(top2, le, AX, ALU.max))
            first_of(le, top2, id2, tmp4)
            V.tensor_tensor(rt[:, 260:265], top2, top1, ALU.subtract).then_inc(sem("rt_shifted"), 1)
            e1, e2 = col(315), col(320)
            for idx, ex in ((id1, e1), (id2, e2)):
                link(V.scalar_tensor_tensor(out=ex, in0=grp, scalar=4.0, in1=idx, op0=ALU.mult, op1=ALU.add))
            oh = mat(0, E)
            ohs = [mat(330, E), mat(410, E)]
            valid = cst[:, C_VT:C_VT + TILES]
            for ex, dst in ((e1, ohs[0]), (e2, ohs[1])):
                link(V.tensor_tensor(dst, i16, b3(ex, E), ALU.is_equal))
                link(V.tensor_tensor(dst, dst, b3(valid, E), ALU.mult))
            V.tensor_tensor(oh, ohs[0], ohs[1], ALU.add).then_inc(sem("onehot_ready"), 1)
            dve.wait_ge(sem("rt_exp"), 1)
            link(V.tensor_reduce(gmax, ge, AX, ALU.add))
            link(V.reciprocal(gmax, gmax))
            dve.wait_ge(sem("rt_exp"), 2)
            ex2 = col(260)
            link(V.tensor_scalar(w1c, ex2, 1.0, None, ALU.add))
            link(V.reciprocal(w1c, w1c))
            link(V.tensor_tensor(w1c, w1c, gmax, ALU.mult))
            link(V.tensor_tensor(w2c, w1c, ex2, ALU.mult))
            dve.wait_ge(sem("pos_mm"), 1)
            cum = mat(80, E)
            link(V.tensor_copy(cum, pb[6][:, 0:TILES * E].rearrange("p (i e) -> p i e", e=E)))
            for k, ex in enumerate((e1, e2)):
                pos = col(490)
                link(V.tensor_tensor(ohs[k], ohs[k], cum, ALU.mult))
                link(V.tensor_reduce(pos, ohs[k], AX, ALU.add))
                link(V.tensor_scalar(pos, pos, -1.0, None, ALU.add))
                tf = col(495)
                link(V.scalar_tensor_tensor(out=tf, in0=pos, scalar=float(E), in1=ex, op0=ALU.mult, op1=ALU.add))
                link(V.tensor_copy(ints[:, 5 * k:5 * k + 5], tf))
                off = col(502)
                link(V.tensor_scalar(off, pos, CAP - 0.5, float(FAR), ALU.is_gt, ALU.mult))
                link(V.tensor_tensor(off, off, pos, ALU.add))
                link(V.scalar_tensor_tensor(out=tf, in0=ex, scalar=float(CAP), in1=off, op0=ALU.mult, op1=ALU.add))
                link(V.tensor_copy(ints[:, 10 + 5 * k:15 + 5 * k], tf))
                link(V.tensor_scalar(off, pos, CAP - 0.5, float(FAR), ALU.is_lt, ALU.mult))
                link(V.tensor_tensor(off, off, pos, ALU.add))
                link(V.tensor_scalar(off, off, -float(CAP), None, ALU.add))
                link(V.scalar_tensor_tensor(out=tf, in0=ex, scalar=float((PASSES - 1) * CAP), in1=off, op0=ALU.mult,
                                            op1=ALU.add))
                link(V.tensor_copy(ints[:, 84 + 5 * k:89 + 5 * k], tf))
            dve.sem_inc(sem("slots_ready"), 1)
            top = rt[:, 500:501]
            link(V.tensor_reduce(top, pb[7][:, 0:E], AX, ALU.max))
            link(V.tensor_scalar(top, top, CAP + 0.5, None, ALU.is_gt))
            V.tensor_copy(ints[:, 80:81], top).then_inc(sem("flag_ready"), 1)
            dve.wait_ge(sem("flag_ready"), 1)

            def turn_mult(e, n, par, turn):
                dve.wait_ge(sem("xt_mm"), n + 1)
                after(dve, "u_mm", n - 1)
                V.tensor_copy(xeT[par][:, 4:8, 0:CAP], pb[1][:, :].rearrange("p (k n) -> p k n", k=4)[:, :, 0:CAP]
                              ).then_inc(sem("xt_ready"), 1)
                dve.wait_ge(sem("u_mm"), n + 1)
                dve.wait_ge(sem("silu"), n + 1)
                after(dve, "y_mm", 2 * n - 2)
                V.tensor_tensor(he[par][:, :, 0:CAP], sg[par][:, :, 0:CAP], pb[3][:, 0:FE * CAP].rearrange("p (f n) -> p f n", f=FE), ALU.mult
                                ).then_inc(sem("h_ready"), 1)

            def y_out(e, n, par, turn):
                dve.wait_ge(sem("y_mm"), 2 * n + 2)
                after(dve, "y_stored%d" % par, 16 * turn)
                V.tensor_copy(ye[par][0:CAP, 512:1024], pb[5][0:CAP, :]).then_inc(sem("y_out"), 1)

            expert_units(0, turn_mult, dve, y_out)
            more = dve.value_load(ints[0:1, 80:81], min_val=0, max_val=1)
            with dve.If(more != 0):
                with dve.Fori(1, PASSES) as b:
                    expert_units(b, turn_mult, dve, y_out)

            wcs = (w1c, w2c)
            for i in range(TILES):
                rows = ROWS[i]
                dve.wait_ge(sem("yg_in%d" % i), 32)
                for k in range(2):
                    ins = V.scalar_tensor_tensor(out=x2[0:rows, i, :], in0=yg[2 * i + k][0:rows, :],
                                                 scalar=wcs[k][0:rows, i:i + 1], in1=x2[0:rows, i, :],
                                                 op0=ALU.mult, op1=ALU.add)
                    if k == 0:
                        link(ins)
                ins.then_inc(sem("x3_ready"), 1)
            dve.wait_ge(sem("x3_sq"), TILES)
            rs = small[:, 32:37]
            link(V.tensor_scalar(rs, rs, 1.0 / D, EPS, ALU.mult, ALU.add))
            V.reciprocal(rs, rs).then_inc(sem("recip"), 1)
            dve.wait_ge(sem("rstd"), 5)
            dve.wait_ge(sem("gf_in"), 16)
            for i in range(TILES):
                rows = ROWS[i]
                V.scalar_tensor_tensor(out=yg[2 * i][0:rows, :], in0=x2[0:rows, i, :], scalar=small[0:rows, 32 + i:33 + i],
                                       in1=gf[0:rows, :], op0=ALU.mult, op1=ALU.mult).then_inc(sem("out_ready"), 1)

        @block.gpsimd
        def _(po):
            def store(dst, src, name, n=16):
                po.dma_start(dst, src).then_inc(sem(name), 16)

            nc.gpsimd.iota(ints[:, 20:25], pattern=[[P, TILES]], base=0, channel_multiplier=1).then_inc(sem("iota"), 1)
            nc.gpsimd.memset(empty[:, :], FAR).then_inc(sem("iota"), 1)
            po.wait_ge(sem("iota"), 2)
            store(scratch_ix.rearrange("(p n) o -> p (n o)", p=P), empty[:, :], "slots_empty")
            cmp_dst = ring[:, 2:4, :].rearrange("p s n -> p (s n)")
            po.wait_ge(sem("pages_in"), 16)
            for s in range(3):
                after(po, "cmp_mm", 2 * s)
                load_pages(po, 32 * s + PAGES, PAGES, t["cmp_pages"], cmp_dst[:, PAGES * 256:], "cmp_in_po", 4)
            po.wait_ge(sem("vn_ready"), 1)
            po.dma_start(o[8], vn[0:NS, PT, :]).then_inc(sem("gmv_out"), 16)
            po.wait_ge(sem("cmp_mm"), 6)
            for i in range(TILES):
                rows = ROWS[i]
                first = PAGES + 3 * i
                load_pages(po, 96 + first, 3, t["cmp_pages"], cmp_dst[:, first * 256:], "cmp_in_po", 3)
                po.wait_ge(sem("proj_out"), BLK_KC * TILES + i + 1)
                dst = o[2][i * P:i * P + P] if i < PT else o[3]
                po.dma_start(dst, stk[0:rows, i % 4, :]).then_inc(sem("kvc_first" if i == 0 else "kvc_out"), 16)
            po.wait_ge(sem("cmp_mm"), 8)
            load_pages(po, PAGES, PAGES, t["sel_pages"], ring[:, SEL_SLOT[1], :], "sel_in1", 4)
            po.wait_ge(sem("proj_done"), 5 * TILES)
            load_pages(po, 3 * PAGES, PAGES, t["sel_pages"], ring[:, SEL_SLOT[3], :], "sel_in3", 4)
            for i in range(TILES):
                rows = ROWS[i]
                dst = o[4][i * P:i * P + P] if i < PT else o[5]
                po.dma_start(dst, kvn[0:rows, i, 0:256]).then_inc(sem("kv_out"), 16)
                po.wait_ge(sem("proj_out"), BLK_KW * TILES + i + 1)
                dst = o[6][i * P:i * P + P] if i < PT else o[7]
                po.dma_start(dst, kvn[0:rows, i, 256:512]).then_inc(sem("kv_out"), 16)
            po.wait_ge(sem("samp_pv"), 1)
            for q in (1, 3):
                load_pages(po, PAGES * (HALF + q), PAGES, t["sel_pages"], ring[:, SEL_SLOT[q], :], "sel_in%d" % q, 4)
            for i in range(TILES):
                rows = ROWS[i]
                po.wait_ge(sem("h2_ready"), i + 1)
                po.dma_start(scratch_h2[i * P:i * P + rows, :], h2[i % 2][0:rows, :]).then_inc(sem("h2_out%d" % (i % 2)), 16)
            po.wait_ge(sem("slots_ready"), 1)
            po.wait_ge(sem("slots_empty"), 16)
            for i in range(TILES):
                for k in range(2):
                    rows = ROWS[i]
                    po.indirect_dma_start(
                        scratch_ix, bass.IndirectOffsetOnAxis(ints[0:rows, 5 * k + i:5 * k + i + 1].bitcast(U32), 0),
                        ints[0:rows, 20 + i:21 + i], None).then_inc(sem("slots_out"), 16)
            po.wait_ge(sem("slots_out"), 16 * 2 * TILES)
            for b in range(PASSES):
                po.dma_start(slot_tokens[0:CAP, E * b:E * b + E],
                             scratch_ix[b * CAP * E:(b + 1) * CAP * E, :].rearrange("(s e) o -> s (e o)", e=E)
                             ).then_inc(sem("slots_back"), 16)
            for k in range(2):
                po.wait_ge(sem("h2_out%d" % k), 16 * (3 - k))
            po.wait_ge(sem("slots_back"), 16 * PASSES)
            po.wait_ge(sem("mix_used"), TILES)
            po.wait_ge(sem("attn_done"), 1)
            for k in range(2):
                nc.gpsimd.memset(xe[k], 0.0).then_inc(sem("xe_zero"), 1)
            po.wait_ge(sem("xe_zero"), 2)

            last_token = po.to_reg(TOK - 1)

            def passes(b):
                def gather(e, par):
                    after(po, "xt_mm", b * E + e - 1)
                    nc.gpsimd.tensor_copy(ints[0:CAP, 82 + par:83 + par], slot_tokens[0:CAP, bass.ds(b * E + e, 1)])
                    po.drain()
                    po.indirect_dma_start(xe[par][0:CAP, :], None, scratch_h2,
                                          bass.IndirectOffsetOnAxis(ints[0:CAP, 82 + par:83 + par].bitcast(U32), 0),
                                          bounds_check=last_token, oob_is_err=False).then_inc(sem("xe_in%d" % par), 16)

                def y_store(e, par):
                    po.wait_ge(sem("y_out"), 2 * (b * E + e) + 2)
                    if isinstance(b, int):
                        dst = scratch_y[bass.ds(e * CAP, CAP), :]
                    else:
                        dst = scratch_z[bass.ds((e * (PASSES - 1) + b - 1) * CAP, CAP), :]
                    po.dma_start(dst, ye[par][0:CAP, :]).then_inc(sem("y_stored%d" % par), 16)

                gather(0, 0)
                gather(1, 1)
                gather(2, 0)
                y_store(0, 0)
                with po.Fori(1, E // 2 - 1) as m:
                    gather(2 * m + 1, 1)
                    y_store(2 * m - 1, 1)
                    gather(2 * m + 2, 0)
                    y_store(2 * m, 0)
                gather(E - 1, 1)
                for e in range(E - 3, E):
                    y_store(e, e % 2)

            def results(table, column, name):
                last_row = po.to_reg(table.shape[0] - 1)
                for i in range(TILES):
                    for k in range(2):
                        at = column + 5 * k + i
                        po.indirect_dma_start(
                            yg[2 * i + k][0:ROWS[i], :], None, table,
                            bass.IndirectOffsetOnAxis(ints[0:ROWS[i], at:at + 1].bitcast(U32), 0),
                            bounds_check=last_row, oob_is_err=False
                        ).then_inc(sem(name if name == "more_in" else name + str(i)), 16)

            passes(0)
            for k in range(2):
                po.wait_ge(sem("y_stored%d" % k), 16 * E // 2)
            po.wait_ge(sem("flag_ready"), 1)
            more = po.value_load(ints[0:1, 80:81], min_val=0, max_val=1)
            with po.If(more != 0):
                with po.Fori(1, PASSES) as b:
                    passes(b)
                for k in range(2):
                    po.wait_ge(sem("y_stored%d" % k), 16 * E // 2 * PASSES)
                results(scratch_z, 84, "more_in")
                po.wait_ge(sem("more_in"), 32 * TILES)
            po.sem_inc(sem("y_all"), 1)
            results(scratch_y, 10, "yg_in")
            po.wait_ge(sem("kvc_first"), 16)
            po.wait_ge(sem("kvc_out"), 16 * (TILES - 1))
            po.wait_ge(sem("kv_out"), 32 * TILES)
            po.wait_ge(sem("gmv_out"), 16)


def _layouts(inp):
    def a(name):
        return np.asarray(inp[name])

    x = np.concatenate([a("x_prompt")[0], a("x_sample").reshape(NS, D)], 0)
    consts, alibi, earlier = constants()
    cmp_kv = a("cache_cmp_kv")[0].reshape(NPOOL, 2, 32, 2, 2, G, HD)
    sel_kv = a("cache_sel_kv")[0].reshape(NPOOL, PAGE, 2, 2 * HD)
    win = a("state_win_kv")[0].reshape(NB, WIN, 2, 2 * HD)
    win_v = win[:, :, 1].reshape(NB, 4, P, P).transpose(0, 2, 1, 3).reshape(NB, P, 512)
    ws = a("w_spatial")[0]
    return {
        "x": x,
        "xT": x.T.reshape(KD, P, TOK).transpose(1, 0, 2).reshape(P, KD * TOK),
        "pages": a("page_table").astype(np.int32).reshape(1, P),
        "consts": consts, "alibi": alibi.reshape(P, 4096), "earlier": earlier,
        "pe": a("pe_cmp")[0].reshape(2, 32, 2, HD).transpose(2, 3, 0, 1).reshape(P, 2, 32),
        "w1": a("w_cmp1")[0].reshape(2, 32, P, P).transpose(2, 0, 1, 3).reshape(P, 2, SLOT),
        "w2": a("w_cmp2")[0].transpose(1, 0, 2),
        "g1": a("norm1_g")[0].reshape(KD, P).T, "gout": a("out_norm_g")[0].reshape(KD, P).T,
        "cmp_pages": cmp_kv.transpose(0, 3, 6, 4, 2, 5, 1).reshape(NPOOL, P, 256),
        "sel_pages": np.concatenate([sel_kv[:, :, 0].transpose(0, 2, 1), sel_kv[:, :, 1]], 2),
        "win": np.concatenate([win[:, :, 0].transpose(0, 2, 1), win_v], 2),
        "ln_g": a("gm_ln_g")[0].reshape(1, 512), "ln_b": a("gm_ln_b")[0].reshape(1, 512),
        "ws_t": ws.transpose(2, 0, 1).reshape(P, GM * P),
        "ws_s": np.tile(ws[:, :NT, :NT].transpose(2, 0, 1), (NB, 1, NB)).reshape(NS, GM * NS),
        "bs_t": a("b_spatial")[0].T, "bs_s": np.tile(a("b_spatial")[0][:, :NT].T, (NB, 1)),
        "w_in": a("w_in")[0], "w_out": a("w_out")[0],
        "w_router": np.concatenate([a("w_router_group")[0], a("w_router_expert")[0]], 1)
        .reshape(KD, P, 20).transpose(1, 0, 2).reshape(P, KD * 20),
        "b_router": np.concatenate([a("b_router_group")[0], a("b_router_expert")[0]]).reshape(1, 20),
        "g2": a("norm2_g")[0].reshape(1, D), "gf": a("final_norm_g").reshape(1, D),
        "w_gate": a("w_gate_e")[0].reshape(E, KD, P, EH).transpose(0, 2, 1, 3).reshape(E, P, SLOT),
        "w_up": a("w_up_e")[0].reshape(E, KD, P, EH).transpose(0, 2, 1, 3).reshape(E, P, SLOT),
        "w_down": a("w_down_e")[0].reshape(E, FE, P, D).transpose(0, 2, 1, 3).reshape(E, P, SLOT),
    }


_OUTS = [(SEQ, D), (NS, D)] + [(SEQ, 256), (NS, 256)] * 3 + [(NS, 512)]
_SHAPES = [(1, SEQ, D), (NB, NT, D)] + [(1, 1, SEQ, 2, G, HD), (1, NB, NT, 2, G, HD)] * 3 + [(1, NB, NT, GM, HD)]


def kernel(**inputs):
    import numpy as _np
    import concourse.bacc as _bacc
    from concourse import mybir as _mybir
    from concourse.bass_utils import run_bass_kernel_spmd as _run

    nc = _bacc.Bacc("TRN2", target_bir_lowering=False, num_devices=1)
    arrays, aps = {}, {}
    for name, a in _layouts(inputs).items():
        a = _np.ascontiguousarray(a)
        arrays[f"in_{name}_dram"] = a
        aps[name] = nc.dram_tensor(f"in_{name}_dram", a.shape, _mybir.dt.from_np(a.dtype), kind="ExternalInput").ap()
    outs = [nc.dram_tensor(f"out_{i}_dram", s, F32, kind="ExternalOutput").ap() for i, s in enumerate(_OUTS)]
    hybrid_layer(nc, aps, outs)
    r = _run(nc, [arrays], core_ids=[0])
    return tuple(r.results[0][f"out_{i}_dram"].reshape(s) for i, s in enumerate(_SHAPES))
```

```python
from contextlib import ExitStack

import numpy as np

import concourse.bass as bass
from concourse import mybir

F32 = mybir.dt.float32
I32 = mybir.dt.int32
U32 = mybir.dt.uint32
ALU = mybir.AluOpType
ACT = mybir.ActivationFunctionType
AX = mybir.AxisListType.X

P = 128
D = 1024
KD = D // P
SEQ = 512
NB, NT = 8, 4
NS = NB * NT
TOK = SEQ + NS
PT = SEQ // P
TILES = PT + 1
ROWS = [P] * PT + [NS]
H, HD, G, HPG = 8, 64, 2, 4
PAST, PAGE, L = 2048, 128, 64
PAGES = PAST // PAGE
BLKS = PAST // L
PBLK = SEQ // L
NSEL = 15
WIN = 512
NPOOL = 160
W = 512
GM = 8
CUT = [(1816, 2328), (1304, 1816), (0, 512), (512, 1024), (1024, 1304)]
BLK_V, BLK_U, BLK_Q, BLK_KC, BLK_KW = range(5)
WIN_SLOT = (4, 5, 4, 5, 4)
WIN_AT = (0, 0, 0, 0, 1024)
SEL_SLOT = (2, 3, 5, 4)
NPROJ = 2328
E, EH = 16, 512
FE = EH // P
CAP = 128
PASSES = -(-TOK // CAP)
EPS = 1e-6
BIG = 1e30
FAR = 1 << 20
HALF = NB // 2
SLOT = 4096
CURW = NS
SELW = PAST + CURW
WINW = WIN + CURW

C_ID, C_ONE, C_TRI, C_HS = 0, 128, 256, 384
C_SG = 512
C_SO = C_SG + 256
C_HM = C_SO + 512
C_GM = C_HM + 24
C_PB = C_GM + 2
C_PM = C_PB + PT * 64
C_SB = C_PM + PT * 64
C_VM = C_SB + BLKS
C_WS = C_VM + H
C_IE = C_WS + NS
C_VT = C_IE + E
C_OF = C_VT + TILES
C_BL = C_OF + L
C_CU = C_BL + BLKS
C_WB = C_CU + CURW
C_ND = C_WB + WIN


def slopes():
    return np.exp2(-np.arange(1, H + 1, dtype=np.float64))


def constants():
    c = np.zeros((P, C_ND), np.float32)
    p = np.arange(P)
    c[:, C_ID:C_ID + P] = np.eye(P)
    c[:, C_ONE:C_ONE + P] = 1
    c[:, C_TRI:C_TRI + P] = p[:, None] <= p[None, :]
    b, g, h, t = p // 32, p // 16 % 2, p // 4 % 4, p % 4
    same = (b[:, None] == b) & (g[:, None] == g) & (t[:, None] == t)
    c[:, C_HS:C_HS + P] = same
    head = g * HPG + h
    slope = slopes()[head]
    for hf in range(2):
        token = (hf * HALF + b) * NT + t
        for r in range(P):
            c[token[r], C_SG + hf * P + r] = 1
            c[r, C_SO + (hf * H + head[r]) * NS + token[r]] = 1
    for br in range(3):
        c[p, C_HM + br * H + head] = 1
    c[p, C_GM + g] = 1
    for i in range(PT):
        for hh in range(H):
            at = i * 64 + hh * PBLK
            dist = (i * P + p)[:, None] - ((np.arange(PBLK) + 1) * L - 1)[None, :]
            c[:, C_PB + at:C_PB + at + PBLK] = np.where(dist >= 0, slopes()[hh] * dist, BIG)
            c[:, C_PM + at:C_PM + at + PBLK] = dist >= 0
    now = PAST + t
    c[:, C_SB:C_SB + BLKS] = slope[:, None] * (now[:, None] - ((np.arange(BLKS) + 1) * L - 1))
    c[p[:64], C_VM + p[:64] // PBLK] = 1
    q = np.arange(NS)
    c[:NS, C_WS:C_WS + NS] = (q[:, None] // NT == q // NT) & (q[:, None] <= q)
    c[:, C_IE:C_IE + E] = np.arange(E)
    for i in range(TILES):
        c[:ROWS[i], C_VT + i] = 1
    c[:, C_OF:C_OF + L] = -slope[:, None] * np.arange(L)
    c[:, C_BL:C_BL + BLKS] = slope[:, None] * (now[:, None] - L * np.arange(BLKS))
    back = t[:, None] - (q % NT)[None, :]
    mine = (q // NT)[None, :] == b[:, None]
    c[:, C_CU:C_CU + NS] = np.where(mine & (back >= 0), slope[:, None] * back, BIG)
    dist = now[:, None] - (PAST - WIN + np.arange(WIN))
    c[:, C_WB:C_WB + WIN] = np.where(dist <= WIN, slope[:, None] * dist, BIG)
    j = np.arange(SEQ)
    back = p[:, None] - (j[None, :] - (SEQ - P))
    alibi = np.stack([np.where(back >= 0, s * back, BIG) for s in slopes()], 1).astype(np.float32)
    i = np.arange(BLKS)
    earlier = (i[None, :] < i[:, None]).astype(np.float32).reshape(1, -1)
    return c, alibi, np.repeat(earlier, P, 0)


def hybrid_layer(nc, t, o):
    scratch_h2 = nc.dram_tensor("h2_rows", (TOK, D), F32, kind="Internal").ap()
    scratch_y = nc.dram_tensor("expert_rows", (E * CAP, D), F32, kind="Internal").ap()
    scratch_z = nc.dram_tensor("more_expert_rows", (E * (PASSES - 1) * CAP, D), F32, kind="Internal").ap()
    scratch_ix = nc.dram_tensor("slot_tokens", (PASSES * CAP * E, 1), I32, kind="Internal").ap()

    with ExitStack() as ctx:
        def sb(name, shape, dt=F32):
            return ctx.enter_context(nc.sbuf_tensor(name, shape, dt))

        sems = {}

        def sem(name):
            if name not in sems:
                sems[name] = ctx.enter_context(nc.semaphore(name))
            return sems[name]

        ring = sb("ring", [P, 6, SLOT])
        xr = sb("xr", [P, 5120])
        qT = sb("qT", [P, HPG, TOK])
        ksT = sb("ksT", [P, TOK])
        kwT = sb("kwT", [P, TOK])
        kvn = sb("kvn", [P, TILES, W])
        ugr = sb("ugr", [P, TILES * W])
        vnr = sb("vnr", [P, TILES * W])
        tabs = sb("tabs", [P, 4096])
        work = sb("work", [P, 3072])
        cst = sb("cst", [P, C_ND])
        gates = sb("gates", [P, TILES, 24])
        qbd = sb("qbd", [P, NB, 32])
        kcs = sb("kcs", [P, NB * BLKS])
        kcp = sb("kcp", [P, PBLK])
        vcp = sb("vcp", [64, W])
        w2 = sb("w2", [P, 2, HD])
        pe = sb("pe", [P, 2, 32])
        peb = sb("peb", [P, 2])
        vec = sb("vec", [P, 2 * KD])
        pages = sb("pages", [1, P], I32)
        small = sb("small", [P, 160])
        osm = sb("osm", [P, 2, HD])
        rt = sb("rt", [P, 512])
        ints = sb("ints", [P, 96], I32)
        empty = tabs[:, 3584:3584 + PASSES * CAP * E // P].bitcast(I32)
        slot_tokens = qbd[:, :, :].rearrange("p b n -> p (b n)")[:, 0:PASSES * E].bitcast(I32)

        def vcs(b):
            r = 32 + 32 * (b // HALF)
            return kvn[r:r + 32, PT, P * (b % HALF):P * (b % HALF) + P]

        pb = [ctx.enter_context(nc.psum_tensor(f"pb{i}", [P, 512], F32)) for i in range(8)]

        ident = cst[:, C_ID:C_ID + P]
        ones = cst[:, C_ONE:C_ONE + P]
        xT = xr[:, 0:KD * TOK].rearrange("p (k n) -> p k n", k=KD)
        sq = [(ugr, vnr)[k // 4][:, (k % 4) * TOK:(k % 4 + 1) * TOK] for k in range(KD)]
        ug = ugr[:, :].rearrange("p (i n) -> p i n", i=TILES)
        vn = vnr[:, :].rearrange("p (i n) -> p i n", i=TILES)
        ov = vn
        rb = work[0:1, 2048:2048 + TOK]
        rtok = rt[:, 352:352 + TILES]
        rsq = rt[:, 357:357 + TILES]
        pacc = work[:, 0:256].rearrange("p (c n) -> p c n", c=2)
        w1 = ring[:, 0:2, :].rearrange("p s (l h) -> p s l h", h=P)
        hc = work[:, 0:1024].rearrange("p (c n) -> p c n", c=2)
        xp = ring[:, 4, 0:1024].rearrange("p (i c l n) -> p c i l n", i=PT, c=2, l=32)
        stg = work[:, 2048:3072].rearrange("p (s n) -> p s n", s=2)
        stk = work[:, 2048:3072].rearrange("p (s n) -> p s n", s=4)
        hp = small[:, 0:32].rearrange("p (c n) -> p c n", c=2)
        hrep = small[:, 32:96]
        lng = tabs[:, 0:512]
        lnb = tabs[:, 512:1024]
        wst = tabs[:, 1024:2048].rearrange("p (g n) -> p g n", g=GM)
        lsq = tabs[:, 2048:2560]
        wss = tabs[0:NS, 2560:2816].rearrange("p (g n) -> p g n", g=GM)
        bst = tabs[:, 2816:2824]
        bss = tabs[0:NS, 2824:2832]
        lst = tabs[:, 2832:2872]

        psel = xr[:, 0:SELW]
        ptsel = xr[:, SELW:SELW + PAST].rearrange("p (c n) -> p c n", c=PAGES)
        pwin = xr[:, SELW + PAST:SELW + PAST + WINW]
        ptwin = work[:, 0:512].rearrange("p (c n) -> p c n", c=4)
        ptcs = work[0:32, 512:640]
        ptcw = work[0:32, 640:768]
        ptc = [work[32 * (hf + 1):32 * (hf + 2), 768:896] for hf in range(2)]
        rank = work[:, 1024:2048].rearrange("p (a b) -> p a b", a=BLKS)
        earlier = work[:, 2048:3072]
        sb3 = [work[:, 512 * k:512 * (k + 1)] for k in range(3)]
        pts = [work[:, 1536 + 512 * k:2048 + 512 * k] for k in range(2)]
        alibi = tabs[:, :].rearrange("p (h n) -> p h n", h=H)
        pcT = rt[0:64, 0:128]
        oT = work[:, 2560:3072]

        mixT = [work[:, 1024 * k:1024 * (k + 1)].rearrange("p (c n) -> p c n", c=KD) for k in range(2)]
        x2 = xr[:, :].rearrange("p (i n) -> p i n", i=TILES)
        g2 = tabs[:, 0:1024]
        h2 = [tabs[:, 1024 * (1 + k):1024 * (2 + k)] for k in range(2)]
        h2T = tabs[:, 3072:4096].rearrange("p (c n) -> p c n", c=KD)
        wr = work[:, 2048:2208].rearrange("p (c n) -> p c n", c=KD)
        br = work[:, 2208:2228]
        xe = [ugr[:, 1024 * k:1024 * (k + 1)] for k in range(2)]
        xeT = [vnr[:, 1024 * k:1024 * (k + 1)].rearrange("p (c n) -> p c n", c=KD) for k in range(2)]
        kvf = kvn[:, :, :].rearrange("p i n -> p (i n)")
        ye = [kvf[:, 1024 * k:1024 * (k + 1)] for k in range(2)]
        qf = qT[:, :, :].rearrange("p i n -> p (i n)")
        he = [qf[:, 512 * k:512 * (k + 1)].rearrange("p (f n) -> p f n", f=FE) for k in range(2)]
        sg = [qf[:, 1024 + 512 * k:1024 + 512 * (k + 1)].rearrange("p (f n) -> p f n", f=FE) for k in range(2)]
        WG, WU, WD = (2, 5), (3, 0), (4, 1)
        yg = [ring[:, 2 + n // 4, 1024 * (n % 4):1024 * (n % 4 + 1)] for n in range(2 * TILES)]
        gf = ring[:, 5, 0:1024]

        def after(eng, name, value):
            if not isinstance(value, int) or value > 0:
                eng.wait_ge(sem(name), value)

        def expert_units(b, first, eng, last):
            def unit(e, half, par):
                return e, b * E + e, par, b * (E // 2) + half

            first(*unit(0, 0, 0))
            first(*unit(1, 0, 1))
            last(*unit(0, 0, 0))
            first(*unit(2, 1, 0))
            last(*unit(1, 0, 1))
            with eng.Fori(1, E // 2 - 1) as m:
                first(*unit(2 * m + 1, m, 1))
                last(*unit(2 * m, m, 0))
                first(*unit(2 * m + 2, m + 1, 0))
                last(*unit(2 * m + 1, m, 1))
            first(*unit(E - 1, E // 2 - 1, 1))
            last(*unit(E - 2, E // 2 - 1, 0))
            last(*unit(E - 1, E // 2 - 1, 1))

        def gsel(hh):
            return slice(64 * (hh // HPG), 64 * (hh // HPG) + 64), hh % HPG

        def load_pages(eng, first, count, table, dst, name, at_once):
            def turn(j):
                for k in range(at_once):
                    page = eng.value_load(pages[0:1, bass.ds(j + first + k, 1)], min_val=0, max_val=NPOOL - 1)
                    eng.dma_start(dst[:, bass.ds(j * 256 + k * 256, 256)],
                                  table[bass.ds(page, 1), :, :].rearrange("o p n -> (o p) n")
                                  ).then_inc(sem(name), 16)

            if count == at_once:
                turn(0)
            else:
                with eng.Fori(0, count // at_once) as m:
                    turn(m * at_once)

        LATE = 3 * TILES

        units = [(i, br_, hh) for i in range(PT) for br_ in range(2) for hh in range(H)]
        CHUNKS = [range(0, 32), range(32, 64)]
        def compressed_at(*lags):
            at = {}
            for i in range(PT):
                for stage, lag in enumerate(lags):
                    at.setdefault(16 * i + (lag if i % 2 else 0), []).append((i, stage))
            return at

        COMPRESSED_PE, COMPRESSED_ACT, COMPRESSED_DVE = (compressed_at(*lags) for lags in
                                                         ((-2, 1, 3), (-1, 0, 3), (-2, 0, 2)))

        block = ctx.enter_context(nc.Block())

        @block.sync
        def _(sp):
            def load(dst, src, name):
                sp.dma_start(dst, src).then_inc(sem(name), 16)

            def w_in(nb):
                a, b = CUT[nb]
                dst = ring[:, WIN_SLOT[nb], WIN_AT[nb]:WIN_AT[nb] + KD * (b - a)].rearrange("p (k n) -> p k n", k=KD)
                load(dst, t["w_in"][:, a:b].rearrange("(k p) n -> p k n", p=P), "win_in%d" % (nb % 2))

            cmp_dst = ring[:, 2:4, :].rearrange("p s n -> p (s n)")
            load(xr[:, 0:KD * TOK], t["xT"], "x_in")
            load(cst[:, :], t["consts"], "cst_in")
            load(pages[:, :], t["pages"], "pages_in")
            load(vec[:, 0:KD], t["g1"], "g1_in")
            w_in(BLK_V)
            load(vec[:, KD:2 * KD], t["gout"], "pe_in")
            load(pe[:, :, :], t["pe"], "pe_in")
            load(w2[:, :, :], t["w2"], "pe_in")
            load(ring[:, 0:2, :], t["w1"], "w1_in")
            sp.wait_ge(sem("pages_in"), 16)
            load_pages(sp, 0, PAGES, t["cmp_pages"], cmp_dst, "cmp_in_sp", 4)
            w_in(BLK_U)
            load(lng, t["ln_g"].to_broadcast([P, 512]), "gm_in")
            load(lnb, t["ln_b"].to_broadcast([P, 512]), "gm_in")
            load(tabs[:, 1024:2048], t["ws_t"], "gm_in")
            load(tabs[0:NS, 2560:2816], t["ws_s"], "gm_in")
            load(bst, t["bs_t"], "gm_in")
            load(bss, t["bs_s"], "gm_in")
            for s in range(1, 4):
                sp.wait_ge(sem("proj_done"), TILES * s)
                w_in(s + 1)
                sp.wait_ge(sem("cmp_mm"), 2 * s)
                first = 32 * s
                load_pages(sp, first, PAGES, t["cmp_pages"], cmp_dst, "cmp_in_sp", 4)
                if s == 3:
                    rest = 2 * PAGES - PAGES - LATE
                    load_pages(sp, first + 2 * PAGES - rest, rest, t["cmp_pages"],
                               cmp_dst[:, (2 * PAGES - rest) * 256:], "cmp_in_sp", rest)

            def selected(hf):
                for q in range(0, HALF, 2):
                    if hf == 0:
                        if q == 0:
                            sp.wait_ge(sem("cmp_mm"), 8)
                        else:
                            sp.wait_ge(sem("proj_done"), TILES * 4)
                    elif q == 0:
                        sp.wait_ge(sem("samp_pv"), 1)
                    load_pages(sp, PAGES * (hf * HALF + q), PAGES, t["sel_pages"], ring[:, SEL_SLOT[q], :],
                               "sel_in%d" % q, 4)
                    if q == 0:
                        load(ring[:, hf, :].rearrange("p (q n) -> p q n", q=HALF),
                             t["win"][hf * HALF:(hf + 1) * HALF].rearrange("q p n -> p q n"), "wst_in%d" % hf)

            selected(0)
            sp.wait_ge(sem("slots_empty"), 16)
            sp.wait_ge(sem("earlier_free"), 1)
            sp.wait_ge(sem("kvc_first"), 16)
            sp.wait_ge(sem("kvc_out"), 16 * (TILES - 1))
            load(earlier, t["earlier"], "earlier_in")
            sp.wait_ge(sem("gm_done"), 1)
            load(tabs[:, :], t["alibi"], "alibi_in")
            selected(1)
            sp.wait_ge(sem("earlier_free"), 2)
            load(earlier, t["earlier"], "earlier_in")
            sp.wait_ge(sem("samp_pv"), 2)
            load(ring[:, 0:2, :].rearrange("p s n -> p (s n)").rearrange("p (k n) -> p k n", k=KD),
                 t["w_out"].rearrange("(k p) n -> p k n", p=P), "wout_in")
            for i in range(TILES):
                load(x2[0:ROWS[i], i, :], t["x"][i * P:i * P + ROWS[i], :], "xnat_in")
            sp.wait_ge(sem("attn_done"), 1)
            load(wr, t["w_router"], "router_in")
            load(br, t["b_router"].to_broadcast([P, 20]), "router_in")
            load(g2, t["g2"].to_broadcast([P, D]), "router_in")

            def slab(name, e):
                if isinstance(e, int):
                    return t[name][e]
                return t[name][bass.ds(e, 1), :, :].rearrange("o p n -> (o p) n")

            def gate(e, n, par, turn):
                after(sp, "g_mm", n - 1)
                load(ring[:, WG[par], :], slab("w_gate", e), "wg_in%d" % par)

            def up(e, n, par, turn):
                after(sp, "u_mm", n - 1)
                load(ring[:, WU[par], :], slab("w_up", e), "wu_in%d" % par)

            def gate_up(e, n, par, turn):
                gate(e, n, par, turn)
                up(e, n, par, turn)

            def down(e, n, par, turn):
                after(sp, "y_mm", 2 * n - 2)
                load(ring[:, WD[par], :], slab("w_down", e), "wd_in%d" % par)

            gate_up(0, 0, 0, 0)
            down(0, 0, 0, 0)
            gate(1, 1, 1, 0)
            sp.wait_ge(sem("out_mm"), 2 * TILES)
            up(1, 1, 1, 0)
            down(1, 1, 1, 0)
            gate_up(2, 2, 0, 1)
            with sp.Fori(1, E // 2 - 1) as m:
                gate_up(2 * m + 1, 2 * m + 1, 1, m)
                down(2 * m, 2 * m, 0, m)
                gate_up(2 * m + 2, 2 * m + 2, 0, m + 1)
                down(2 * m + 1, 2 * m + 1, 1, m)
            gate_up(E - 1, E - 1, 1, E // 2 - 1)
            down(E - 2, E - 2, 0, E // 2 - 1)
            down(E - 1, E - 1, 1, E // 2 - 1)
            sp.wait_ge(sem("flag_ready"), 1)
            more = sp.value_load(ints[0:1, 80:81], min_val=0, max_val=1)
            with sp.If(more != 0):
                with sp.Fori(1, PASSES) as b:
                    expert_units(b, gate_up, sp, down)
            sp.wait_ge(sem("y_all"), 1)
            load(gf, t["gf"].to_broadcast([P, D]), "gf_in")
            for i in range(TILES):
                sp.wait_ge(sem("out_ready"), i + 1)
                dst = o[0][i * P:(i + 1) * P, :] if i < PT else o[1]
                sp.dma_start(dst, yg[2 * i][0:ROWS[i], :]).then_inc(sem("stored"), 16)
            sp.wait_ge(sem("stored"), 16 * TILES)

        @block.tensor
        def _(te):
            def mm(out, lhsT, rhs, start=True, stop=True):
                return nc.tensor.matmul(out, lhsT, rhs, start=start, stop=stop)

            te.wait_ge(sem("cst_in"), 16)
            for k in range(KD):
                te.wait_ge(sem("sq_ready"), k + 1)
                for n in range(2):
                    ins = mm(pb[4 + n][:, 0:272], ones, sq[k][:, 272 * n:272 * (n + 1)], k == 0, k == KD - 1)
            ins.then_inc(sem("ss_mm"), 1)

            def position_bias():
                te.wait_ge(sem("pacc_ready"), 1)
                for c in range(2):
                    ins = mm(pb[7][:, c:c + 1], pacc[:, c, :], ones[:, 0:1])
                ins.then_inc(sem("peb_mm"), 1)
                te.wait_ge(sem("peb_ready"), 1)

            def compress(s):
                last = s == 3
                te.wait_ge(sem("cmp_in_sp"), 16 * (5 * PAGES - LATE if last else PAGES * (s + 1)))
                te.wait_ge(sem("cmp_in_po"), 16 * (3 * PAGES + LATE if last else PAGES * (s + 1)))
                if s >= 1:
                    te.wait_ge(sem("hc_ready"), 2 * s)
                count = 2 * PAGES
                if last:
                    te.wait_ge(sem("turn_out"), 2 * TILES)
                    count += PT
                raw = ring[:, 2:5, :].rearrange("p s n -> p (s n)")[:, 0:256 * count].rearrange(
                    "p (j c l n) -> p c l j n", j=count, c=2, l=32)
                for c in range(2):
                    for l in range(32):
                        ins = mm(pb[6 + c][:, 0:4 * count], w1[:, c, l, :], raw[:, c, l, :, :], l == 0, l == 31)
                    ins.then_inc(sem("cmp_mm"), 1)

            def compress_last():
                te.wait_ge(sem("hc_ready"), 8)
                te.wait_ge(sem("pcmp_h"), 2)
                hcv = hc.rearrange("p c (j g n) -> p c j g n", g=G, n=2)
                for g in range(G):
                    mm(pb[6][64 * g:64 * g + 64, 0:256], w2[:, 0, :], hcv[:, 0, :, g, :])
                for b in range(NB):
                    for g in range(G):
                        r = 32 * (b // HALF)
                        ins = mm(pb[7][r:r + 32, 128 * (b % HALF) + 64 * g:128 * (b % HALF) + 64 * g + 64],
                                 hc[:, 1, 64 * b + 32 * g:64 * b + 32 * g + 32], w2[:, 1, :])
                ins.then_inc(sem("comp_mm"), 1)

            turn = {BLK_Q: 4, BLK_KC: 3, BLK_KW: 1}

            def project(n):
                nb, i = divmod(n, TILES)
                a, b = CUT[nb]
                if i == 0:
                    te.wait_ge(sem("win_in%d" % (nb % 2)), 16 * (nb // 2 + 1))
                if n >= 4:
                    te.wait_ge(sem("proj_out"), n - 3)
                wv = ring[:, WIN_SLOT[nb], WIN_AT[nb]:WIN_AT[nb] + KD * (b - a)].rearrange("p (k n) -> p k n", k=KD)
                for k in range(KD):
                    ins = mm(pb[n % 4][0:ROWS[i], 0:b - a], xT[:, k, i * P:i * P + ROWS[i]], wv[:, k, :],
                             k == 0, k == KD - 1)
                ins.then_inc(sem("proj_done"), 1)

            def turned(n):
                nb, i = divmod(n, TILES)
                rows = ROWS[i]
                t = n - BLK_Q * TILES
                te.wait_ge(sem("proj_out"), n + 1)
                if t >= 2:
                    te.wait_ge(sem("turn_out"), t - 1)
                bank = pb[4 + t % 2]
                for m in range(turn[nb]):
                    if nb == BLK_Q:
                        src = stg[0:rows, n % 2, 128 * m:128 * m + 128]
                    elif nb == BLK_KC:
                        src = stk[0:rows, i % 4, 128 * m:128 * m + 128] if m < 2 else kvn[0:rows, i, 0:128]
                    else:
                        src = kvn[0:rows, i, 256:384]
                    ins = nc.tensor.transpose(bank[:, 128 * m:128 * m + rows], src, ident[0:rows, 0:rows])
                ins.then_inc(sem("turned"), 1)

            def block_of(nb):
                for n in range(nb * TILES, (nb + 1) * TILES):
                    project(n)
                    if nb >= BLK_Q and n % TILES:
                        turned(n - 1)
                if nb >= BLK_Q:
                    turned(n)

            te.wait_ge(sem("xg_ready"), KD)
            project(0)
            te.wait_ge(sem("rstd"), 1)
            for i in range(TILES):
                ins = mm(pb[6][0:ROWS[i], i:i + 1], rb[:, P * i:P * i + ROWS[i]], ones[0:1, 0:1])
            ins.then_inc(sem("rs_mm"), 1)
            for n in range(1, TILES):
                project(n)
            position_bias()
            te.wait_ge(sem("rs_ready"), 1)
            compress(0)
            block_of(BLK_U)
            compress(1)
            block_of(BLK_Q)
            te.wait_ge(sem("proj_out"), 3 * TILES)
            te.wait_ge(sem("turn_out"), TILES)
            te.wait_ge(sem("vn_ready"), 1)
            te.wait_ge(sem("ws_ready"), 2)
            for g in range(GM):
                mm(pb[g // 2][:, 256 * (g % 2):256 * (g % 2) + 256], wst[:, g, :], vn[:, 0:PT, 64 * g:64 * g + 64])
                ins = mm(pb[4][0:NS, 64 * g:64 * g + 64], wss[:, g, :], vn[0:NS, PT, 64 * g:64 * g + 64])
            ins.then_inc(sem("gm_mm"), 1)
            compress(2)
            te.wait_ge(sem("gm_done"), 1)
            block_of(BLK_KC)
            compress(3)
            block_of(BLK_KW)
            compress_last()
            te.wait_ge(sem("turn_out"), 3 * TILES)
            te.wait_ge(sem("hrep_ready"), 1)
            te.wait_ge(sem("pcmp_h"), 2)
            for g in range(G):
                mm(pb[4][64 * g:64 * g + 64, 0:PBLK], w2[:, 0, :], hp[:, 0, PBLK * g:PBLK * (g + 1)])
            ins = mm(pb[4][0:64, 64:128], hrep, w2[:, 1, :])
            ins.then_inc(sem("pcomp_mm"), 1)

            def sampled(hf):
                te.wait_ge(sem("qbd_ready"), 1)
                if hf == 0:
                    te.wait_ge(sem("proj_out"), 5 * TILES)
                    te.wait_ge(sem("pcomp_ready"), 2)
                    te.wait_ge(sem("comp_ready"), 2)
                else:
                    te.wait_ge(sem("combined"), 4)
                    te.wait_ge(sem("pcv_ready"), 2)
                for q in range(HALF):
                    b = hf * HALF + q
                    r = slice(32 * q, 32 * q + 32)
                    ins = mm(pb[5][r, 0:32], qbd[:, b, :], kcs[:, 32 * b:32 * b + 32])
                    mm(pb[5][r, 64:96], qbd[:, b, :], kwT[:, SEQ:TOK])
                    ins = mm(pb[5][r, 96:128], qbd[:, b, :], ksT[:, SEQ:TOK])
                ins.then_inc(sem("samp_scores"), 1)
                te.wait_ge(sem("wst_in%d" % hf), 16)
                for q in range(HALF):
                    mm(pb[4][32 * q:32 * q + 32, :], qbd[:, hf * HALF + q, :], ring[:, hf, 1024 * q:1024 * q + 512])
                te.wait_ge(sem("gate_ready"), 1)
                ins = mm(pb[7][:, 0:24], cst[0:32, C_SG + hf * P:C_SG + (hf + 1) * P], gates[0:32, PT, :])
                ins.then_inc(sem("samp_scores"), 1)
                te.wait_ge(sem("pc_norm"), hf + 1)
                mm(pb[7][:, 32:64], cst[:, C_HS:C_HS + P], small[:, 96:128]).then_inc(sem("imp_mm"), 1)
                nc.tensor.transpose(pb[6][0:32, 0:128], small[:, 96:128], ident)
                for q in range(HALF):
                    slot = SEL_SLOT[q]
                    te.wait_ge(sem("sel_in%d" % q), 16 * PAGES * (hf + 1))
                    kt = ring[:, slot, :].rearrange("p (j n) -> p j n", j=PAGES)
                    for m in range(4):
                        ins = mm(pb[m][32 * q:32 * q + 32, :], qbd[:, hf * HALF + q, :], kt[:, 4 * m:4 * m + 4, 0:128])
                ins.then_inc(sem("samp_scores"), 1)
                te.wait_ge(sem("pw_ready"), hf + 1)
                for m in range(4):
                    nc.tensor.transpose(pb[4][:, 128 * m:128 * m + 128], pwin[:, 128 * m:128 * m + 128], ident)
                nc.tensor.transpose(pb[6][0:32, 128:256], pwin[:, WIN:WINW], ident).then_inc(sem("samp_tw"), 1)
                te.wait_ge(sem("ps_ready"), hf + 1)
                for m in range(PAGES):
                    ins = nc.tensor.transpose(pb[m // 4][:, 128 * (m % 4):128 * (m % 4) + 128],
                                              psel[:, 128 * m:128 * m + 128], ident)
                    if m % 4 == 3:
                        ins.then_inc(sem("samp_ts"), 1)
                nc.tensor.transpose(pb[7][0:32, 384:512], psel[:, PAST:SELW], ident).then_inc(sem("samp_ts"), 1)
                te.wait_ge(sem("samp_pt0"), 2 * hf + 2)
                for q in range(HALF):
                    b = hf * HALF + q
                    r = slice(32 * q, 32 * q + 32)
                    mm(pb[5][r, 0:128], ptc[hf][:, r], vcs(b))
                    for m in range(4):
                        mm(pb[6][r, 256:384], ptwin[:, m, r], ring[:, hf, 1024 * q + 512 + 128 * m:1024 * q + 640 + 128 * m],
                           m == 0, False)
                    mm(pb[6][r, 256:384], ptcw[:, r], kvn[0:32, PT, 384:512], False, True)
                te.wait_ge(sem("samp_pts"), 5 * hf + 5)
                for q in range(HALF):
                    slot = SEL_SLOT[q]
                    r = slice(32 * q, 32 * q + 32)
                    for m in range(PAGES):
                        mm(pb[6][r, 128:256], ptsel[:, m, r], ring[:, slot, 256 * m + 128:256 * m + 256], m == 0, False)
                    ins = mm(pb[6][r, 128:256], ptcs[:, r], kvn[0:32, PT, 128:256], False, True)
                ins.then_inc(sem("samp_pv"), 1)

            def prompt_compressed(i, stage):
                if stage == 0:
                    if i >= 1:
                        te.wait_ge(sem("pcv_ready"), i)
                        te.wait_ge(sem("combined"), 2 * i - 1)
                    for hh in range(H):
                        r, h = gsel(hh)
                        bank = (pb[4], pb[7])[hh // HPG]
                        ins = mm(bank[:, 8 * hh:8 * hh + 8], qT[r, h, i * P:i * P + P], kcp[r, :])
                    ins.then_inc(sem("pcs_mm"), 1)
                elif stage == 1:
                    te.wait_ge(sem("pcp_ready"), i + 1)
                    nc.tensor.transpose(pb[7][0:64, 0:128], small[:, 0:64], ident).then_inc(sem("pct_mm"), 1)
                else:
                    te.wait_ge(sem("pct_out"), i + 1)
                    mm(pb[4][:, :], pcT, vcp[:, :]).then_inc(sem("pcv_mm"), 1)

            def scores(u):
                i, b, hh = units[u]
                n = P * (i + 1)
                r, h = gsel(hh)
                if u >= 2:
                    te.wait_ge(sem("biased"), u - 1)
                kt = (ksT, kwT)[b]
                mm(pb[u % 2][:, 0:n], qT[r, h, i * P:i * P + P], kt[r, 0:n]).then_inc(sem("score_mm"), 1)

            def turn_probs(u):
                i = units[u][0]
                te.wait_ge(sem("probs"), u + 1)
                if u >= 2:
                    te.wait_ge(sem("pt_out"), u - 1)
                for m in range(i + 1):
                    ins = nc.tensor.transpose(pb[2 + u % 2][:, P * m:P * m + P], sb3[u % 3][:, P * m:P * m + P], ident)
                ins.then_inc(sem("pt_mm"), 1)

            def values(u):
                i, b, hh = units[u]
                te.wait_ge(sem("pt_out"), u + 1)
                if u == CHUNKS[0][0]:
                    te.wait_ge(sem("samp_o"), 1)
                elif u == CHUNKS[1][0]:
                    te.wait_ge(sem("samp_o"), 2)
                pair = u // H
                if hh == 0 and pair >= 2:
                    te.wait_ge(sem("oT_ready"), pair - 1)
                r, h = gsel(hh)
                col = 128 + 256 * b + 64 * (hh // HPG)
                for m in range(i + 1):
                    ins = mm(pb[5 + b][r, P * h:P * h + P], kvn[:, m, col:col + 64],
                             pts[u % 2][:, P * m:P * m + P], m == 0, m == i)
                ins.then_inc(sem("pv_mm"), 1)

            def turn_results(pair):
                te.wait_ge(sem("oT_ready"), pair + 1)
                te.wait_ge(sem("pct_out"), pair // 2 + 1)
                if pair >= 1:
                    te.wait_ge(sem("combined"), pair)
                for h in range(HPG):
                    ins = nc.tensor.transpose(pb[7][:, P * h:P * h + P], oT[:, P * h:P * h + P], ident)
                ins.then_inc(sem("o_turned"), 1)

            def prompt(chunk):
                end = chunk[-1]
                for v in range(chunk[0], end + 5):
                    for i, stage in COMPRESSED_PE.get(v, ()) if v <= end else ():
                        prompt_compressed(i, stage)
                    if v <= end:
                        scores(v)
                    if chunk[0] <= v - 2 <= end:
                        turn_probs(v - 2)
                    if chunk[0] <= v - 3 <= end:
                        values(v - 3)
                    if chunk[0] <= v - 4 and (v - 4) % H == H - 1:
                        turn_results((v - 4) // H)

            sampled(0)
            prompt(CHUNKS[0])
            sampled(1)
            prompt(CHUNKS[1])
            te.wait_ge(sem("combined"), 8)
            te.wait_ge(sem("samp_o"), 2)
            for hh in range(H):
                for hf in range(2):
                    at = C_SO + (hf * H + hh) * NS
                    ins = mm(pb[0][0:NS, 64 * hh:64 * hh + 64], cst[:, at:at + NS], osm[:, hf, :], hf == 0, hf == 1)
            ins.then_inc(sem("osamp_mm"), 1)

            def mix_turn(i):
                te.wait_ge(sem("mix_ready"), i + 1)
                if i >= 1:
                    te.wait_ge(sem("mixT_ready"), 8 * i)
                rows = ROWS[i]
                for k in range(KD):
                    src = (ov, ug)[k // 4][0:rows, i, P * (k % 4):P * (k % 4) + P]
                    ins = nc.tensor.transpose(pb[k // 4][:, P * (k % 4):P * (k % 4) + rows], src,
                                              ident[0:rows, 0:rows])
                ins.then_inc(sem("mix_used"), 1)

            wo = ring[:, 0:2, :].rearrange("p s n -> p (s n)").rearrange("p (k n) -> p k n", k=KD)

            def out_product(i):
                te.wait_ge(sem("mixT_ready"), 8 * (i + 1))
                te.wait_ge(sem("wout_in"), 16)
                for n in range(2):
                    j = 2 * i + n
                    if j >= 3:
                        te.wait_ge(sem("x2_ready"), j - 2)
                    for k in range(KD):
                        ins = mm(pb[4 + j % 3][0:ROWS[i], :], mixT[i % 2][:, k, 0:ROWS[i]],
                                 wo[:, k, W * n:W * n + W], k == 0, k == KD - 1)
                    ins.then_inc(sem("out_mm"), 1)

            def turn_normed(i):
                rows = ROWS[i]
                te.wait_ge(sem("h2_ready"), i + 1)
                if i >= 1:
                    te.wait_ge(sem("h2T_ready"), 2 * i)
                for k in range(KD):
                    ins = nc.tensor.transpose(pb[2 + k // 4][:, P * (k % 4):P * (k % 4) + rows],
                                              h2[i % 2][0:rows, P * k:P * k + P], ident[0:rows, 0:rows])
                ins.then_inc(sem("h2_turned"), 1)

            def router(i):
                rows = ROWS[i]
                te.wait_ge(sem("h2T_ready"), 2 * (i + 1))
                if i >= 1:
                    te.wait_ge(sem("logit_out"), i)
                for k in range(KD):
                    ins = mm(pb[7][0:rows, 0:20], h2T[:, k, 0:rows], wr[:, k, :], k == 0, k == KD - 1)
                ins.then_inc(sem("logit_mm"), 1)

            te.wait_ge(sem("router_in"), 48)
            for i in range(TILES + 3):
                if i < TILES:
                    mix_turn(i)
                if i >= 3:
                    router(i - 3)
                if 1 <= i <= TILES:
                    out_product(i - 1)
                if 2 <= i < TILES + 2:
                    turn_normed(i - 2)
            te.wait_ge(sem("x2_ready"), 2 * TILES)
            te.wait_ge(sem("logit_out"), TILES)
            te.wait_ge(sem("onehot_ready"), 1)
            oh = rt[:, 0:TILES * E].rearrange("p (i e) -> p i e", e=E)
            for i in range(TILES):
                for j in range(i):
                    mm(pb[6][:, E * i:E * i + E], ones, oh[:, j, :], j == 0, False)
                mm(pb[6][:, E * i:E * i + E], cst[:, C_TRI:C_TRI + P], oh[:, i, :], i == 0, True)
            for j in range(TILES):
                ins = mm(pb[7][:, 0:E], ones, oh[:, j, :], j == 0, j == TILES - 1)
            ins.then_inc(sem("pos_mm"), 1)

            def gate_up(e, n, par, turn):
                te.wait_ge(sem("xe_in%d" % par), 16 * (turn + 1))
                after(te, "xt_ready", 2 * n)
                for k in range(KD):
                    ins = nc.tensor.transpose(pb[k // 4][:, P * (k % 4):P * (k % 4) + CAP],
                                              xe[par][0:CAP, P * k:P * k + P], ident[0:CAP, 0:CAP])
                ins.then_inc(sem("xt_mm"), 1)
                te.wait_ge(sem("xt_ready"), 2 * n + 2)
                after(te, "h_ready", n)
                for slots, bank, weights, done in ((WG, 2, "wg_in", "g_mm"), (WU, 3, "wu_in", "u_mm")):
                    te.wait_ge(sem(weights + "%d" % par), 16 * (turn + 1))
                    wv = ring[:, slots[par], :].rearrange("p (k f) -> p k f", k=KD)
                    for f in range(FE):
                        for k in range(KD):
                            ins = mm(pb[bank][:, CAP * f:CAP * f + CAP], wv[:, k, P * f:P * f + P],
                                     xeT[par][:, k, 0:CAP], k == 0, k == KD - 1)
                    ins.then_inc(sem(done), 1)

            def down(e, n, par, turn):
                te.wait_ge(sem("h_ready"), n + 1)
                te.wait_ge(sem("wd_in%d" % par), 16 * (turn + 1))
                after(te, "y_out", 2 * n)
                wv = ring[:, WD[par], :].rearrange("p (f n) -> p f n", f=FE)
                for c in range(2):
                    for f in range(FE):
                        ins = mm(pb[4 + c][0:CAP, :], he[par][:, f, 0:CAP], wv[:, f, W * c:W * c + W], f == 0, f == FE - 1)
                    ins.then_inc(sem("y_mm"), 1)

            expert_units(0, gate_up, te, down)
            te.wait_ge(sem("flag_ready"), 1)
            more = te.value_load(ints[0:1, 80:81], min_val=0, max_val=1)
            with te.If(more != 0):
                with te.Fori(1, PASSES) as b:
                    expert_units(b, gate_up, te, down)

        @block.scalar
        def _(act):
            A = nc.scalar.activation
            act.wait_ge(sem("x_in"), 16)
            for k in range(KD):
                A(sq[k], xT[:, k, :], ACT.Square).then_inc(sem("sq_ready"), 1)
            act.wait_ge(sem("recip"), 1)
            A(rb, rb, ACT.Sqrt).then_inc(sem("rstd"), 1)

            def compress(s):
                for c in range(2):
                    act.wait_ge(sem("cmp_mm"), 2 * s + c + 1)
                    bank = pb[6 + c]
                    if c == 0:
                        A(hc[:, c, P * s:P * s + P], bank[:, 0:128], ACT.Gelu_apprx_tanh,
                          bias=peb[:, c:c + 1]).then_inc(sem("hc_ready"), 1)
                        continue
                    for b in range(2):
                        at = P * s + 64 * b
                        ins = A(hc[:, c, at:at + 64].rearrange("p (g j n) -> p j g n", g=G, n=2),
                                bank[:, 64 * b:64 * b + 64].rearrange("p (j g n) -> p j g n", g=G, n=2),
                                ACT.Gelu_apprx_tanh, bias=peb[:, c:c + 1])
                    ins.then_inc(sem("hc_ready"), 1)

            def projected(n):
                nb, i = divmod(n, TILES)
                rows = ROWS[i]
                act.wait_ge(sem("proj_done"), n + 1)
                bank = pb[n % 4]
                if nb <= BLK_U:
                    A((vn, ug)[nb][0:rows, i, :], bank[0:rows, :], ACT.Gelu_apprx_tanh, scale=rtok[0:rows, i:i + 1]).then_inc(sem("proj_out"), 1)
                elif nb == BLK_Q:
                    if i >= 2:
                        act.wait_ge(sem("turned"), i - 1)
                    for g in range(G):
                        ins = A(stg[0:rows, n % 2, :].rearrange("p (h g d) -> p g h d", h=HPG, g=G)[:, g],
                                bank[0:rows, :].rearrange("p (g h d) -> p g h d", h=HPG, g=G)[:, g],
                                ACT.Copy, scale=rsq[0:rows, i:i + 1])
                    ins.then_inc(sem("proj_out"), 1)
                elif nb == BLK_KC:
                    if i == 0:
                        act.wait_ge(sem("turned"), TILES)
                    elif i == 4:
                        act.wait_ge(sem("turned"), TILES + 1)
                        act.wait_ge(sem("kvc_first"), 16)
                    A(stk[0:rows, i % 4, :], bank[0:rows, 0:256], ACT.Copy, scale=rtok[0:rows, i:i + 1])
                    A(kvn[0:rows, i, 0:256], bank[0:rows, 256:512], ACT.Copy, scale=rtok[0:rows, i:i + 1]).then_inc(sem("proj_out"), 1)
                else:
                    A(kvn[0:rows, i, 256:512], bank[0:rows, 0:256], ACT.Copy, scale=rtok[0:rows, i:i + 1])
                    A(gates[0:rows, i, :], bank[0:rows, 256:280], ACT.Copy, scale=rtok[0:rows, i:i + 1]).then_inc(sem("proj_out"), 1)

            def block_of(nb):
                for n in range(nb * TILES, (nb + 1) * TILES):
                    projected(n)

            act.wait_ge(sem("rs_ready"), 1)
            block_of(BLK_V)
            act.wait_ge(sem("peb_mm"), 1)
            nc.scalar.copy(peb[:, :], pb[7][:, 0:2]).then_inc(sem("peb_ready"), 1)
            act.wait_ge(sem("peb_ready"), 1)
            compress(0)
            block_of(BLK_U)
            compress(1)
            act.wait_ge(sem("recip"), 2)
            A(lst, lst, ACT.Sqrt).then_inc(sem("rstd"), 1)
            block_of(BLK_Q)
            compress(2)
            act.wait_ge(sem("gm_done"), 1)
            for i in range(TILES):
                A(ov[0:ROWS[i], i, :], ug[0:ROWS[i], i, :], ACT.Square,
                  accum_out=rt[0:ROWS[i], 362 + i:363 + i]).then_inc(sem("mix_sq"), 1)
            block_of(BLK_KC)
            compress(3)
            for c in range(2):
                A(hp[:, c, :].rearrange("p (g i b) -> p i g b", g=G, i=PT),
                  pb[6 + c][:, 128:144].rearrange("p (i g b) -> p i g b", g=G, i=PT), ACT.Gelu_apprx_tanh,
                  bias=peb[:, c:c + 1]).then_inc(sem("pcmp_h"), 1)
            act.wait_ge(sem("gates_zero"), 1)
            block_of(BLK_KW)
            act.wait_ge(sem("proj_out"), 5 * TILES)
            A(gates[:, :, :], gates[:, :, :], ACT.Exp, scale=-1.0).then_inc(sem("gate_exp"), 1)
            act.wait_ge(sem("comp_mm"), 1)
            for n in range(2):
                ins = nc.scalar.copy(kvn[32 + 32 * n:64 + 32 * n, PT, :], pb[7][32 * n:32 * n + 32, :])
            ins.then_inc(sem("comp_ready"), 1)

            def sampled(hf):
                act.wait_ge(sem("samp_biased"), 3 * hf + 1)
                A(small[:, 96:128], small[:, 96:128], ACT.Exp, scale=-1.0, bias=small[:, 128:129],
                  accum_out=small[:, 131:132]).then_inc(sem("pc_exp"), 1)
                act.wait_ge(sem("samp_biased"), 3 * hf + 2)
                A(pwin, pwin, ACT.Exp, scale=-1.0, bias=small[:, 130:131],
                  accum_out=small[:, 133:134]).then_inc(sem("pw_ready"), 1)
                act.wait_ge(sem("samp_tw"), hf + 1)
                nc.scalar.copy(ptc[hf], pb[6][0:32, 0:128])
                nc.scalar.copy(ptwin.rearrange("p c n -> p (c n)"), pb[4][:, :]).then_inc(sem("samp_pt0"), 1)
                nc.scalar.copy(ptcw, pb[6][0:32, 128:256]).then_inc(sem("samp_pt0"), 1)
                act.wait_ge(sem("samp_biased"), 3 * hf + 3)
                A(psel, psel, ACT.Exp, scale=-1.0, bias=small[:, 129:130],
                  accum_out=small[:, 132:133]).then_inc(sem("ps_ready"), 1)

            def compressed(i, stage):
                if stage == 0:
                    act.wait_ge(sem("pcx_ready"), i + 1)
                    A(small[:, 0:64], small[:, 0:64], ACT.Exp, scale=-1.0).then_inc(sem("pce_ready"), 1)
                elif stage == 2:
                    act.wait_ge(sem("pcv_mm"), i + 1)
                    nc.scalar.copy(ov[:, i, :], pb[4][:, :]).then_inc(sem("pcv_ready"), 1)

            def exponentials(u):
                i, b, hh = units[u]
                n = P * (i + 1)
                if hh == 0 and u >= 16:
                    act.wait_ge(sem("combined"), u // H - 1)
                act.wait_ge(sem("biased"), u + 1)
                A(sb3[u % 3][:, 0:n], sb3[u % 3][:, 0:n], ACT.Exp, scale=-1.0, bias=rt[:, 128 + u % 4:129 + u % 4],
                  accum_out=rt[:, 136 + 8 * (u // H % 2) + hh:137 + 8 * (u // H % 2) + hh]).then_inc(sem("probs"), 1)

            def results_out(pair):
                act.wait_ge(sem("pv_mm"), H * (pair + 1))
                after(act, "o_turned", pair)
                nc.scalar.copy(oT, pb[5 + pair % 2][:, :]).then_inc(sem("oT_ready"), 1)

            def prompt(chunk):
                end = chunk[-1]
                for v in range(chunk[0], end + 4):
                    for i, stage in COMPRESSED_ACT.get(v, ()) if v <= end else ():
                        compressed(i, stage)
                    if v <= end:
                        exponentials(v)
                    if chunk[0] <= v - 3 and (v - 3) % H == H - 1:
                        results_out((v - 3) // H)

            sampled(0)
            prompt(CHUNKS[0])
            sampled(1)
            prompt(CHUNKS[1])
            act.wait_ge(sem("attn_done"), 1)
            for i in range(TILES):
                if i == PT:
                    act.wait_ge(sem("osamp_mm"), 1)
                    nc.scalar.copy(ov[0:NS, PT, :], pb[0][0:NS, :]).then_inc(sem("osamp_out"), 1)
                    act.wait_ge(sem("osamp_out"), 1)
                act.wait_ge(sem("mix_sq"), TILES + i)
                A(work[0:ROWS[i], 2560:3072], ov[0:ROWS[i], i, :], ACT.Square,
                  accum_out=rt[0:ROWS[i], 367 + i:368 + i]).then_inc(sem("mix_sq"), 1)
            act.wait_ge(sem("recip"), 3)
            A(rt[:, 362:372], rt[:, 362:372], ACT.Sqrt).then_inc(sem("rstd"), 1)

            def mixed(i):
                act.wait_ge(sem("mix_used"), i + 1)
                if i >= 2:
                    act.wait_ge(sem("out_mm"), 2 * (i - 1))
                for k in range(KD):
                    A(mixT[i % 2][:, k, 0:ROWS[i]], pb[k // 4][:, P * (k % 4):P * (k % 4) + ROWS[i]],
                      ACT.Copy, scale=vec[:, KD + k:KD + k + 1]).then_inc(sem("mixT_ready"), 1)

            def norm_of(i):
                for n in range(2):
                    act.wait_ge(sem("x2_ready"), 2 * i + n + 1)
                    after(act, "x2_sq", 2 * i + n)
                    A(work[0:ROWS[i], 2560:3072], x2[0:ROWS[i], i, W * n:W * n + W], ACT.Square,
                      accum_out=small[0:ROWS[i], 16 + 2 * i + n:17 + 2 * i + n]).then_inc(sem("x2_sq"), 1)
                act.wait_ge(sem("recip"), 4 + i)
                A(small[:, 48 + i:49 + i], small[:, 48 + i:49 + i], ACT.Sqrt).then_inc(sem("rstd"), 1)

            def rows_turned(i):
                act.wait_ge(sem("h2_turned"), i + 1)
                after(act, "logit_mm", i)
                nc.scalar.copy(h2T[:, 0:4, 0:ROWS[i]],
                               pb[2][:, :].rearrange("p (k n) -> p k n", k=4)[:, :, 0:ROWS[i]]).then_inc(sem("h2T_ready"), 1)

            for i in range(TILES + 2):
                if i < TILES:
                    mixed(i)
                if i >= 2:
                    rows_turned(i - 2)
                if 1 <= i <= TILES:
                    norm_of(i - 1)
            act.wait_ge(sem("rt_shifted"), 1)
            A(rt[:, 220:240], rt[:, 220:240], ACT.Exp).then_inc(sem("rt_exp"), 1)
            act.wait_ge(sem("rt_shifted"), 2)
            A(rt[:, 260:265], rt[:, 260:265], ACT.Exp).then_inc(sem("rt_exp"), 1)

            def turn_silu(e, n, par, turn):
                act.wait_ge(sem("xt_mm"), n + 1)
                after(act, "u_mm", n - 1)
                nc.scalar.copy(xeT[par][:, 0:4, 0:CAP], pb[0][:, :].rearrange("p (k n) -> p k n", k=4)[:, :, 0:CAP]
                               ).then_inc(sem("xt_ready"), 1)
                act.wait_ge(sem("g_mm"), n + 1)
                after(act, "h_ready", n - 1)
                A(sg[par][:, :, 0:CAP], pb[2][:, 0:FE * CAP].rearrange("p (f n) -> p f n", f=FE), ACT.Silu).then_inc(sem("silu"), 1)

            def y_out(e, n, par, turn):
                act.wait_ge(sem("y_mm"), 2 * n + 1)
                after(act, "y_stored%d" % par, 16 * turn)
                nc.scalar.copy(ye[par][0:CAP, 0:512], pb[4][0:CAP, :]).then_inc(sem("y_out"), 1)

            expert_units(0, turn_silu, act, y_out)
            act.wait_ge(sem("flag_ready"), 1)
            more = act.value_load(ints[0:1, 80:81], min_val=0, max_val=1)
            with act.If(more != 0):
                with act.Fori(1, PASSES) as b:
                    expert_units(b, turn_silu, act, y_out)
            for i in range(TILES + 1):
                if i < TILES:
                    act.wait_ge(sem("x3_ready"), i + 1)
                    A(yg[2 * i + 1][0:ROWS[i], :], x2[0:ROWS[i], i, :], ACT.Square,
                      accum_out=small[0:ROWS[i], 32 + i:33 + i]).then_inc(sem("x3_sq"), 1)
                if i >= 1:
                    act.wait_ge(sem("recip"), 3 + TILES + i)
                    A(small[:, 31 + i:32 + i], small[:, 31 + i:32 + i], ACT.Sqrt).then_inc(sem("rstd"), 1)

        @block.vector
        def _(dve):
            V = nc.vector
            chain = [0]

            def link(ins):
                chain[0] += 1
                ins.then_inc(sem("dve_step"), 1)
                dve.wait_ge(sem("dve_step"), chain[0])

            V.memset(gates[:, :, :], 0.0).then_inc(sem("gates_zero"), 1)
            link(V.memset(qbd[:, :, :], 0.0))
            link(V.memset(rt[:, :], 0.0))
            link(V.memset(small[:, :], 1.0))
            dve.wait_ge(sem("g1_in"), 16)
            for k in range(KD):
                dve.wait_ge(sem("sq_ready"), k + 1)
                V.tensor_scalar(xT[:, k, :], xT[:, k, :], vec[:, k:k + 1], None, ALU.mult).then_inc(sem("xg_ready"), 1)
            dve.wait_ge(sem("ss_mm"), 1)
            for n in range(2):
                link(V.tensor_scalar(rb[:, 272 * n:272 * n + 272], pb[4 + n][0:1, 0:272], 1.0 / D, EPS, ALU.mult, ALU.add))
            V.reciprocal(rb, rb).then_inc(sem("recip"), 1)
            dve.wait_ge(sem("rs_mm"), 1)
            link(V.tensor_copy(rtok[:, 0:PT], pb[6][:, 0:PT]))
            link(V.tensor_copy(rtok[0:NS, PT:TILES], pb[6][0:NS, PT:TILES]))
            link(V.tensor_scalar(rsq, rtok, -(HD ** -0.5), None, ALU.mult))
            dve.sem_inc(sem("rs_ready"), 1)
            dve.wait_ge(sem("pe_in"), 48)
            dve.wait_ge(sem("w1_in"), 16)
            for l in range(32):
                for c in range(2):
                    if l == 0:
                        ins = V.tensor_scalar(pacc[:, c, :], w1[:, c, l, :], pe[:, c, l:l + 1], None, ALU.mult)
                    else:
                        ins = V.scalar_tensor_tensor(out=pacc[:, c, :], in0=w1[:, c, l, :], scalar=pe[:, c, l:l + 1],
                                                     in1=pacc[:, c, :], op0=ALU.mult, op1=ALU.add)
                link(ins)
            dve.sem_inc(sem("pacc_ready"), 1)
            def turned(t):
                nb, i = divmod(t + BLK_Q * TILES, TILES)
                rows = ROWS[i]
                dve.wait_ge(sem("turned"), t + 1)
                bank = pb[4 + t % 2]
                if nb == BLK_Q:
                    ins = V.tensor_copy(qT[:, :, i * P:i * P + rows],
                                        bank[:, :].rearrange("p (h n) -> p h n", h=HPG)[:, :, 0:rows])
                elif nb == BLK_KC:
                    if i < PT:
                        for c in range(2):
                            src = bank[:, 128 * c:128 * c + 128].rearrange("p (b l q) -> p q l b", b=2, q=2)
                            for g in range(G):
                                for q in range(2):
                                    V.tensor_copy(xp[64 * q:64 * q + 64, c, i, :, 2 * g:2 * g + 2],
                                                  src[64 * g:64 * g + 64, q, :, :])
                    ins = V.tensor_copy(ksT[:, i * P:i * P + rows], bank[:, 256:256 + rows])
                else:
                    ins = V.tensor_copy(kwT[:, i * P:i * P + rows], bank[:, 128 * 0:rows])
                ins.then_inc(sem("turn_out"), 1)
                if t == TILES - 1:
                    dve.wait_ge(sem("turn_out"), TILES)
                    for g in range(G):
                        ins = V.tensor_copy(
                            qbd[64 * g:64 * g + 64, :, 16 * g:16 * g + 16].rearrange("p b (h n) -> p b h n", h=HPG),
                            qT[64 * g:64 * g + 64, :, SEQ:TOK].rearrange("p h (b n) -> p b h n", b=NB))
                        ins.then_inc(sem("qbd_part"), 1)
                    dve.wait_ge(sem("qbd_part"), 2)
                    dve.sem_inc(sem("qbd_ready"), 1)

            dve.wait_ge(sem("gm_in"), 96)
            dve.wait_ge(sem("cst_in"), 16)
            link(V.memset(lst, 1.0))
            for i in range(TILES):
                rows = ROWS[i]
                dve.wait_ge(sem("proj_out"), i + 1)
                v = vn[0:rows, i, :].rearrange("p (g d) -> p g d", g=GM)
                mean, var = small[0:rows, 136:144], lst[0:rows, 8 * i:8 * i + 8]
                link(V.tensor_reduce(mean, v, AX, ALU.add))
                link(V.tensor_scalar(mean, mean, 1.0 / HD, None, ALU.mult))
                link(V.tensor_tensor(v, v, mean[:, :, None].to_broadcast([rows, GM, HD]), ALU.subtract))
                s2 = lsq[0:rows, :].rearrange("p (g d) -> p g d", g=GM)
                link(V.tensor_tensor(s2, v, v, ALU.mult))
                link(V.tensor_reduce(var, s2, AX, ALU.add))
            link(V.tensor_scalar(lst, lst, 1.0 / HD, EPS, ALU.mult, ALU.add))
            V.reciprocal(lst, lst).then_inc(sem("recip"), 1)
            V.tensor_tensor(wst, wst, cst[:, C_TRI:C_TRI + P][:, None, :].to_broadcast([P, GM, P]), ALU.mult
                            ).then_inc(sem("ws_ready"), 1)
            V.tensor_tensor(wss, wss, cst[0:NS, C_WS:C_WS + NS][:, None, :].to_broadcast([NS, GM, NS]), ALU.mult
                            ).then_inc(sem("ws_ready"), 1)
            dve.wait_ge(sem("rstd"), 2)
            for i in range(TILES):
                rows = ROWS[i]
                v = vn[0:rows, i, :].rearrange("p (g d) -> p g d", g=GM)
                r = lst[0:rows, 8 * i:8 * i + 8]
                link(V.tensor_tensor(v, v, r[:, :, None].to_broadcast([rows, GM, HD]), ALU.mult))
                link(V.tensor_tensor(vn[0:rows, i, :], vn[0:rows, i, :], lng[0:rows, :], ALU.mult))
                link(V.tensor_tensor(vn[0:rows, i, :], vn[0:rows, i, :], lnb[0:rows, :], ALU.add))
            dve.sem_inc(sem("vn_ready"), 1)
            for t in range(TILES):
                turned(t)
            dve.wait_ge(sem("gm_mm"), 1)
            dve.wait_ge(sem("proj_out"), 2 * TILES)
            for g in range(GM):
                u = ug[:, 0:PT, 64 * g:64 * g + 64]
                src = pb[g // 2][:, 256 * (g % 2):256 * (g % 2) + 256].rearrange("p (c d) -> p c d", c=PT)
                V.scalar_tensor_tensor(out=u, in0=src, scalar=bst[:, g:g + 1], in1=u, op0=ALU.add, op1=ALU.mult)
                u = ug[0:NS, PT, 64 * g:64 * g + 64]
                ins = V.scalar_tensor_tensor(out=u, in0=pb[4][0:NS, 64 * g:64 * g + 64], scalar=bss[:, g:g + 1], in1=u,
                                             op0=ALU.add, op1=ALU.mult)
            link(ins)
            dve.wait_ge(sem("gmv_out"), 16)
            dve.sem_inc(sem("gm_done"), 1)
            for t in range(TILES, 2 * TILES):
                turned(t)
            dve.wait_ge(sem("pcmp_h"), 2)
            V.tensor_copy(hrep.rearrange("p (g h n) -> p g h n", g=G, h=HPG),
                          hp[:, 1, :].rearrange("p (g n) -> p g n", g=G)[:, :, None, :].to_broadcast([P, G, HPG, PBLK])
                          ).then_inc(sem("hrep_ready"), 1)
            for t in range(2 * TILES, 3 * TILES):
                turned(t)
            dve.wait_ge(sem("comp_mm"), 1)
            V.tensor_copy(kcs[:, :], pb[6][:, 0:256]).then_inc(sem("comp_ready"), 1)
            dve.wait_ge(sem("pcomp_mm"), 1)
            V.tensor_copy(kcp[:, :], pb[4][:, 0:PBLK]).then_inc(sem("pcomp_ready"), 1)
            link(V.tensor_copy(small[0:64, 96:160], pb[4][0:64, 64:128]))
            V.tensor_tensor(vcp[:, :].rearrange("p (h d) -> p h d", h=H),
                            small[0:64, 96:160][:, None, :].to_broadcast([64, H, HD]),
                            cst[0:64, C_VM:C_VM + H][:, :, None].to_broadcast([64, H, HD]), ALU.mult
                            ).then_inc(sem("pcomp_ready"), 1)
            dve.wait_ge(sem("gate_exp"), 1)
            gall = gates[:, :, :].rearrange("p i n -> p (i n)")
            link(V.tensor_scalar(gall, gall, 1.0, None, ALU.add))
            link(V.reciprocal(gall, gall))
            dve.sem_inc(sem("gate_ready"), 1)
            dve.sem_inc(sem("earlier_free"), 1)

            mc, ms, mw = (small[:, 128 + k:129 + k] for k in range(3))
            lc, ls, lw = (small[:, 131 + k:132 + k] for k in range(3))
            m2 = small[:, 134:135]
            gr = small[:, 136:139]
            pc = small[:, 96:128]

            def ttr(out, a, b, acc):
                return V.tensor_tensor_reduce(out, a, b, 1.0, 3.0e38, ALU.add, ALU.min, acc)

            def sampled(hf):
                cur = small[:, 0:32]
                link(V.memset(cur, BIG))
                link(V.tensor_copy(cur[:, 16 * hf:16 * hf + 16], cst[:, C_CU:C_CU + 16]))
                s3 = psel[:, 0:PAST].rearrange("p (b l) -> p b l", b=BLKS)
                link(V.tensor_tensor(s3, cst[:, C_BL:C_BL + BLKS][:, :, None].to_broadcast([P, BLKS, L]),
                                     cst[:, C_OF:C_OF + L][:, None, :].to_broadcast([P, BLKS, L]), ALU.add))
                dve.wait_ge(sem("samp_scores"), 3 * hf + 1)
                ttr(pc, pb[5][:, 0:32], cst[:, C_SB:C_SB + BLKS], mc).then_inc(sem("samp_biased"), 1)
                dve.wait_ge(sem("samp_scores"), 3 * hf + 2)
                link(ttr(pwin[:, 0:WIN], pb[4][:, :], cst[:, C_WB:C_WB + WIN], mw))
                link(ttr(pwin[:, WIN:WINW], pb[5][:, 64:96], cur, m2))
                V.tensor_tensor(mw, mw, m2, ALU.min).then_inc(sem("samp_biased"), 1)
                m3 = small[:, 135:136]
                link(ttr(psel[:, PAST:SELW], pb[5][:, 96:128], cur, m3))
                t24 = small[:, 32:56]
                link(V.tensor_tensor(t24, pb[7][:, 0:24], cst[:, C_HM:C_HM + 24], ALU.mult))
                link(V.tensor_reduce(gr, t24.rearrange("p (b h) -> p b h", b=3), AX, ALU.add))
                dve.wait_ge(sem("pc_exp"), hf + 1)
                link(V.reciprocal(lc, lc))
                V.tensor_scalar(pc, pc, lc, None, ALU.mult).then_inc(sem("pc_norm"), 1)
                imp = small[:, 56:88]
                dve.wait_ge(sem("imp_mm"), hf + 1)
                link(V.tensor_copy(imp, pb[7][:, 32:64]))
                other = imp[:, None, :].to_broadcast([P, BLKS, BLKS])
                own = imp[:, :, None].to_broadcast([P, BLKS, BLKS])
                r1, r2 = rt[:, 160:192], rt[:, 192:224]
                link(V.tensor_tensor(rank, other, own, ALU.is_gt))
                link(V.tensor_reduce(r1, rank, AX, ALU.add))
                link(V.tensor_tensor(rank, other, own, ALU.is_equal))
                dve.wait_ge(sem("earlier_in"), 16 * (hf + 1))
                link(V.tensor_tensor(rank, rank, earlier.rearrange("p (a b) -> p a b", a=BLKS), ALU.mult))
                link(V.tensor_reduce(r2, rank, AX, ALU.add))
                link(V.tensor_tensor(r1, r1, r2, ALU.add))
                link(V.tensor_scalar(r1, r1, NSEL - 0.5, BIG, ALU.is_gt, ALU.mult))
                dve.wait_ge(sem("samp_scores"), 3 * hf + 3)
                for m in range(4):
                    ins = V.tensor_tensor(psel[:, 512 * m:512 * m + 512], pb[m][:, :], psel[:, 512 * m:512 * m + 512], ALU.add)
                link(ins)
                link(ttr(s3, s3, r1[:, :, None].to_broadcast([P, BLKS, L]), ms))
                V.tensor_tensor(ms, ms, m3, ALU.min).then_inc(sem("samp_biased"), 1)
                for m in range(4):
                    dve.wait_ge(sem("samp_ts"), 5 * hf + m + 1)
                    V.tensor_copy(ptsel[:, 4 * m:4 * m + 4, :].rearrange("p c n -> p (c n)"), pb[m][:, :]
                                  ).then_inc(sem("samp_pts"), 1)
                dve.wait_ge(sem("samp_ts"), 5 * hf + 5)
                V.tensor_copy(ptcs, pb[7][0:32, 384:512]).then_inc(sem("samp_pts"), 1)
                dve.wait_ge(sem("ps_ready"), hf + 1)
                link(V.reciprocal(small[:, 132:134], small[:, 132:134]))
                link(V.tensor_tensor(gr[:, 1:3], gr[:, 1:3], small[:, 132:134], ALU.mult))
                dve.wait_ge(sem("samp_pv"), hf + 1)
                acc = rt[:, 224:352]
                link(V.tensor_scalar(acc, pb[5][:, 0:128], gr[:, 0:1], None, ALU.mult))
                for m in (1, 2):
                    link(V.scalar_tensor_tensor(out=acc, in0=pb[6][:, 128 * m:128 * m + 128], scalar=gr[:, m:m + 1],
                                                in1=acc, op0=ALU.mult, op1=ALU.add))
                link(V.tensor_scalar(osm[:, hf, :], acc[:, 0:64], cst[:, C_GM:C_GM + 1], None, ALU.mult))
                V.scalar_tensor_tensor(out=osm[:, hf, :], in0=acc[:, 64:128], scalar=cst[:, C_GM + 1:C_GM + 2],
                                       in1=osm[:, hf, :], op0=ALU.mult, op1=ALU.add).then_inc(sem("samp_o"), 1)
                dve.wait_ge(sem("samp_o"), hf + 1)

            def bias(u):
                i, b, hh = units[u]
                n = P * (i + 1)
                dve.wait_ge(sem("score_mm"), u + 1)
                if u >= 3:
                    dve.wait_ge(sem("pt_mm"), u - 2)
                ttr(sb3[u % 3][:, 0:n], pb[u % 2][:, 0:n], alibi[:, hh, SEQ - n:SEQ], rt[:, 128 + u % 4:129 + u % 4]
                    ).then_inc(sem("biased"), 1)

            def probs_out(u):
                n = P * (units[u][0] + 1)
                dve.wait_ge(sem("pt_mm"), u + 1)
                if u >= 2:
                    dve.wait_ge(sem("pv_mm"), u - 1)
                V.tensor_copy(pts[u % 2][:, 0:n], pb[2 + u % 2][:, 0:n]).then_inc(sem("pt_out"), 1)

            def compressed(i, stage):
                x = small[:, 0:64]
                x3 = x.rearrange("p (h n) -> p h n", h=H)
                mx, sm = small[:, 64:72], small[:, 72:80]
                if stage == 0:
                    dve.wait_ge(sem("pcs_mm"), i + 1)
                    for g in range(G):
                        at = C_PB + 64 * i + 32 * g
                        ins = V.tensor_tensor(x[:, 32 * g:32 * g + 32], (pb[4], pb[7])[g][:, 32 * g:32 * g + 32],
                                              cst[:, at:at + 32], ALU.add)
                    link(ins)
                    link(V.tensor_reduce(mx, x3, AX, ALU.min))
                    V.tensor_tensor(x3, x3, mx[:, :, None].to_broadcast([P, H, PBLK]), ALU.subtract
                                    ).then_inc(sem("pcx_ready"), 1)
                elif stage == 1:
                    dve.wait_ge(sem("pce_ready"), i + 1)
                    link(V.tensor_reduce(sm, x3, AX, ALU.add))
                    link(V.reciprocal(sm, sm))
                    link(V.tensor_tensor(sm, sm, gates[:, i, 0:8], ALU.mult))
                    link(V.tensor_tensor(x, x, cst[:, C_PM + 64 * i:C_PM + 64 * i + 64], ALU.mult))
                    V.tensor_tensor(x3, x3, sm[:, :, None].to_broadcast([P, H, PBLK]), ALU.mult
                                    ).then_inc(sem("pcp_ready"), 1)
                else:
                    dve.wait_ge(sem("pct_mm"), i + 1)
                    if i >= 1:
                        dve.wait_ge(sem("pcv_mm"), i)
                    V.tensor_copy(rt[0:64, 0:128], pb[7][0:64, 0:128]).then_inc(sem("pct_out"), 1)

            def combine(pair):
                i, b = divmod(pair, 2)
                dve.wait_ge(sem("probs"), H * (pair + 1))
                if b == 0:
                    dve.wait_ge(sem("pcv_ready"), i + 1)
                at = 136 + 8 * (pair % 2)
                ri = rt[:, 152:160]
                link(V.reciprocal(ri, rt[:, at:at + 8]))
                link(V.tensor_tensor(ri, ri, gates[:, i, 8 + 8 * b:16 + 8 * b], ALU.mult))
                dve.wait_ge(sem("o_turned"), pair + 1)
                for hh in range(H):
                    v = ov[:, i, HD * hh:HD * hh + HD]
                    at = P * (hh % HPG) + HD * (hh // HPG)
                    ins = V.scalar_tensor_tensor(out=v, in0=pb[7][:, at:at + HD], scalar=ri[:, hh:hh + 1], in1=v,
                                                 op0=ALU.mult, op1=ALU.add)
                ins.then_inc(sem("combined"), 1)
                dve.wait_ge(sem("combined"), pair + 1)

            def prompt(chunk):
                end = chunk[-1]
                for v in range(chunk[0], end + 6):
                    for i, stage in COMPRESSED_DVE.get(v, ()) if v <= end else ():
                        compressed(i, stage)
                    if v <= end:
                        bias(v)
                    if chunk[0] <= v - 2 <= end:
                        probs_out(v - 2)
                    if chunk[0] <= v - 5 and (v - 5) % H == H - 1:
                        combine((v - 5) // H)

            sampled(0)
            dve.wait_ge(sem("alibi_in"), 16)
            prompt(CHUNKS[0])
            dve.sem_inc(sem("earlier_free"), 1)
            sampled(1)
            prompt(CHUNKS[1])
            link(V.memset(small[:, 0:64], 1.0))
            dve.sem_inc(sem("attn_done"), 1)

            dve.wait_ge(sem("mix_sq"), 2 * TILES)
            rs = rt[:, 362:372]
            link(V.tensor_scalar(rs, rs, 1.0 / W, EPS, ALU.mult, ALU.add))
            V.reciprocal(rs, rs).then_inc(sem("recip"), 1)
            dve.wait_ge(sem("rstd"), 3)
            for i in range(TILES):
                rows = ROWS[i]
                for m in range(2):
                    v = (ov, ug)[m][0:rows, i, :]
                    ins = V.tensor_scalar(v, v, rt[0:rows, 367 - 5 * m + i:368 - 5 * m + i], None, ALU.mult)
                    if m == 0:
                        link(ins)
                ins.then_inc(sem("mix_ready"), 1)
            dve.wait_ge(sem("xnat_in"), 16 * TILES)
            dve.wait_ge(sem("router_in"), 48)
            lg = rt[:, 80:180].rearrange("p (i n) -> p i n", i=TILES)
            link(V.memset(rt[:, 80:180], 0.0))

            def residual(i):
                rows = ROWS[i]
                for n in range(2):
                    dve.wait_ge(sem("out_mm"), 2 * i + n + 1)
                    v = x2[0:rows, i, W * n:W * n + W]
                    V.tensor_tensor(v, pb[4 + (2 * i + n) % 3][0:rows, :], v, ALU.add).then_inc(sem("x2_ready"), 1)
                dve.wait_ge(sem("x2_sq"), 2 * i + 2)
                rs = small[:, 48 + i:49 + i]
                link(V.tensor_tensor(rs, small[:, 16 + 2 * i:17 + 2 * i], small[:, 17 + 2 * i:18 + 2 * i], ALU.add))
                link(V.tensor_scalar(rs, rs, 1.0 / D, EPS, ALU.mult, ALU.add))
                V.reciprocal(rs, rs).then_inc(sem("recip"), 1)
                dve.wait_ge(sem("rstd"), 4 + i)
                if i >= 2:
                    dve.wait_ge(sem("h2_turned"), i - 1)
                    dve.wait_ge(sem("h2_out%d" % (i % 2)), 16 * (i // 2))
                V.scalar_tensor_tensor(out=h2[i % 2][0:rows, :], in0=x2[0:rows, i, :],
                                       scalar=rs[0:rows, :], in1=g2[0:rows, :],
                                       op0=ALU.mult, op1=ALU.mult).then_inc(sem("h2_ready"), 1)

            def routed(i):
                rows = ROWS[i]
                dve.wait_ge(sem("h2_turned"), i + 1)
                after(dve, "logit_mm", i)
                V.tensor_copy(h2T[:, 4:8, 0:rows],
                              pb[3][:, :].rearrange("p (k n) -> p k n", k=4)[:, :, 0:rows]).then_inc(sem("h2T_ready"), 1)
                dve.wait_ge(sem("logit_mm"), i + 1)
                V.tensor_tensor(lg[0:rows, i, :], pb[7][0:rows, 0:20], br[0:rows, :], ALU.add
                                ).then_inc(sem("logit_out"), 1)

            for i in range(TILES + 1):
                if i >= 1:
                    routed(i - 1)
                if i < TILES:
                    residual(i)
            dve.wait_ge(sem("logit_out"), TILES)

            def b3(x, n):
                return x[:, :, None].to_broadcast([P, TILES, n])

            def col(a):
                return rt[:, a:a + TILES]

            def mat(a, n):
                return rt[:, a:a + TILES * n].rearrange("p (i n) -> p i n", n=n)

            i4 = cst[:, C_IE:C_IE + 4][:, None, :].to_broadcast([P, TILES, 4])
            i16 = cst[:, C_IE:C_IE + E][:, None, :].to_broadcast([P, TILES, E])

            def first_of(x, top, idx, tmp):
                link(V.tensor_tensor(tmp, x, b3(top, 4), ALU.not_equal))
                link(V.tensor_scalar(tmp, tmp, 16.0, None, ALU.mult))
                link(V.tensor_tensor(tmp, tmp, i4, ALU.add))
                link(V.tensor_reduce(idx, tmp, AX, ALU.min))

            lgg = lg[:, :, 0:4]
            gmax, grp, tmp4 = col(180), col(185), mat(190, 4)
            link(V.tensor_reduce(gmax, lgg, AX, ALU.max))
            first_of(lgg, gmax, grp, tmp4)
            ge = mat(220, 4)
            V.tensor_tensor(ge, lgg, b3(gmax, 4), ALU.subtract).then_inc(sem("rt_shifted"), 1)
            oh4, le = mat(240, 4), mat(265, 4)
            link(V.tensor_tensor(oh4, i4, b3(grp, 4), ALU.is_equal))
            link(V.memset(rt[:, 265:285], 0.0))
            for g in range(4):
                link(V.tensor_tensor(tmp4, lg[:, :, 4 + 4 * g:8 + 4 * g], oh4[:, :, g:g + 1].to_broadcast([P, TILES, 4]),
                                     ALU.mult))
                link(V.tensor_tensor(le, le, tmp4, ALU.add))
            top1, top2, id1, id2, w1c, w2c = (col(285 + 5 * k) for k in range(6))
            link(V.tensor_reduce(top1, le, AX, ALU.max))
            first_of(le, top1, id1, tmp4)
            link(V.tensor_tensor(tmp4, i4, b3(id1, 4), ALU.is_equal))
            link(V.tensor_scalar(tmp4, tmp4, -BIG, None, ALU.mult))
            link(V.tensor_tensor(le, le, tmp4, ALU.add))
            link(V.tensor_reduce(top2, le, AX, ALU.max))
            first_of(le, top2, id2, tmp4)
            V.tensor_tensor(rt[:, 260:265], top2, top1, ALU.subtract).then_inc(sem("rt_shifted"), 1)
            e1, e2 = col(315), col(320)
            for idx, ex in ((id1, e1), (id2, e2)):
                link(V.scalar_tensor_tensor(out=ex, in0=grp, scalar=4.0, in1=idx, op0=ALU.mult, op1=ALU.add))
            oh = mat(0, E)
            ohs = [mat(330, E), mat(410, E)]
            valid = cst[:, C_VT:C_VT + TILES]
            for ex, dst in ((e1, ohs[0]), (e2, ohs[1])):
                link(V.tensor_tensor(dst, i16, b3(ex, E), ALU.is_equal))
                link(V.tensor_tensor(dst, dst, b3(valid, E), ALU.mult))
            V.tensor_tensor(oh, ohs[0], ohs[1], ALU.add).then_inc(sem("onehot_ready"), 1)
            dve.wait_ge(sem("rt_exp"), 1)
            link(V.tensor_reduce(gmax, ge, AX, ALU.add))
            link(V.reciprocal(gmax, gmax))
            dve.wait_ge(sem("rt_exp"), 2)
            ex2 = col(260)
            link(V.tensor_scalar(w1c, ex2, 1.0, None, ALU.add))
            link(V.reciprocal(w1c, w1c))
            link(V.tensor_tensor(w1c, w1c, gmax, ALU.mult))
            link(V.tensor_tensor(w2c, w1c, ex2, ALU.mult))
            dve.wait_ge(sem("pos_mm"), 1)
            cum = mat(80, E)
            link(V.tensor_copy(cum, pb[6][:, 0:TILES * E].rearrange("p (i e) -> p i e", e=E)))
            poss, tf, off = (col(490), col(495)), col(500), col(505)
            for k, ex in enumerate((e1, e2)):
                pos = poss[k]
                link(V.tensor_tensor(ohs[k], ohs[k], cum, ALU.mult))
                link(V.tensor_reduce(pos, ohs[k], AX, ALU.add))
                link(V.tensor_scalar(pos, pos, -1.0, None, ALU.add))
                link(V.scalar_tensor_tensor(out=tf, in0=pos, scalar=float(E), in1=ex, op0=ALU.mult, op1=ALU.add))
                link(V.tensor_copy(ints[:, 5 * k:5 * k + 5], tf))
                dve.sem_inc(sem("slots_ready"), 1)
            for k, ex in enumerate((e1, e2)):
                pos = poss[k]
                link(V.tensor_scalar(off, pos, CAP - 0.5, float(FAR), ALU.is_gt, ALU.mult))
                link(V.tensor_tensor(off, off, pos, ALU.add))
                link(V.scalar_tensor_tensor(out=tf, in0=ex, scalar=float(CAP), in1=off, op0=ALU.mult, op1=ALU.add))
                link(V.tensor_copy(ints[:, 10 + 5 * k:15 + 5 * k], tf))
                link(V.tensor_scalar(off, pos, CAP - 0.5, float(FAR), ALU.is_lt, ALU.mult))
                link(V.tensor_tensor(off, off, pos, ALU.add))
                link(V.tensor_scalar(off, off, -float(CAP), None, ALU.add))
                link(V.scalar_tensor_tensor(out=tf, in0=ex, scalar=float((PASSES - 1) * CAP), in1=off, op0=ALU.mult,
                                            op1=ALU.add))
                link(V.tensor_copy(ints[:, 84 + 5 * k:89 + 5 * k], tf))
            top = rt[:, 511:512]
            link(V.tensor_reduce(top, pb[7][:, 0:E], AX, ALU.max))
            link(V.tensor_scalar(top, top, CAP + 0.5, None, ALU.is_gt))
            V.tensor_copy(ints[:, 80:81], top).then_inc(sem("flag_ready"), 1)
            dve.wait_ge(sem("flag_ready"), 1)

            def turn_mult(e, n, par, turn):
                dve.wait_ge(sem("xt_mm"), n + 1)
                after(dve, "u_mm", n - 1)
                V.tensor_copy(xeT[par][:, 4:8, 0:CAP], pb[1][:, :].rearrange("p (k n) -> p k n", k=4)[:, :, 0:CAP]
                              ).then_inc(sem("xt_ready"), 1)
                dve.wait_ge(sem("u_mm"), n + 1)
                dve.wait_ge(sem("silu"), n + 1)
                after(dve, "y_mm", 2 * n - 2)
                V.tensor_tensor(he[par][:, :, 0:CAP], sg[par][:, :, 0:CAP], pb[3][:, 0:FE * CAP].rearrange("p (f n) -> p f n", f=FE), ALU.mult
                                ).then_inc(sem("h_ready"), 1)

            def y_out(e, n, par, turn):
                dve.wait_ge(sem("y_mm"), 2 * n + 2)
                after(dve, "y_stored%d" % par, 16 * turn)
                V.tensor_copy(ye[par][0:CAP, 512:1024], pb[5][0:CAP, :]).then_inc(sem("y_out"), 1)

            expert_units(0, turn_mult, dve, y_out)
            more = dve.value_load(ints[0:1, 80:81], min_val=0, max_val=1)
            with dve.If(more != 0):
                with dve.Fori(1, PASSES) as b:
                    expert_units(b, turn_mult, dve, y_out)

            wcs = (w1c, w2c)
            def combined_rows(i):
                rows = ROWS[i]
                dve.wait_ge(sem("yg_in%d" % i), 32)
                for k in range(2):
                    ins = V.scalar_tensor_tensor(out=x2[0:rows, i, :], in0=yg[2 * i + k][0:rows, :],
                                                 scalar=wcs[k][0:rows, i:i + 1], in1=x2[0:rows, i, :],
                                                 op0=ALU.mult, op1=ALU.add)
                    if k == 0:
                        link(ins)
                ins.then_inc(sem("x3_ready"), 1)

            def mean_square(i):
                dve.wait_ge(sem("x3_sq"), i + 1)
                rs = small[:, 32 + i:33 + i]
                link(V.tensor_scalar(rs, rs, 1.0 / D, EPS, ALU.mult, ALU.add))
                V.reciprocal(rs, rs).then_inc(sem("recip"), 1)

            def last_norm(i):
                rows = ROWS[i]
                dve.wait_ge(sem("rstd"), 4 + TILES + i)
                V.scalar_tensor_tensor(out=yg[2 * i][0:rows, :], in0=x2[0:rows, i, :], scalar=small[0:rows, 32 + i:33 + i],
                                       in1=gf[0:rows, :], op0=ALU.mult, op1=ALU.mult).then_inc(sem("out_ready"), 1)

            dve.wait_ge(sem("gf_in"), 16)
            for i in range(TILES + 1):
                if i < TILES:
                    combined_rows(i)
                if i >= 1:
                    mean_square(i - 1)
                    last_norm(i - 1)

        @block.gpsimd
        def _(po):
            def store(dst, src, name, n=16):
                po.dma_start(dst, src).then_inc(sem(name), 16)

            nc.gpsimd.iota(ints[:, 20:25], pattern=[[P, TILES]], base=0, channel_multiplier=1).then_inc(sem("iota"), 1)
            nc.gpsimd.memset(empty[:, :], FAR).then_inc(sem("iota"), 1)
            po.wait_ge(sem("iota"), 2)
            store(scratch_ix.rearrange("(p n) o -> p (n o)", p=P), empty[:, :], "slots_empty")
            cmp_dst = ring[:, 2:4, :].rearrange("p s n -> p (s n)")
            po.wait_ge(sem("pages_in"), 16)
            for s in range(3):
                after(po, "cmp_mm", 2 * s)
                load_pages(po, 32 * s + PAGES, PAGES, t["cmp_pages"], cmp_dst[:, PAGES * 256:], "cmp_in_po", 4)
            po.wait_ge(sem("vn_ready"), 1)
            po.dma_start(o[8], vn[0:NS, PT, :]).then_inc(sem("gmv_out"), 16)
            po.wait_ge(sem("cmp_mm"), 6)
            for i in range(TILES):
                rows = ROWS[i]
                first = PAGES + 3 * i
                load_pages(po, 96 + first, 3, t["cmp_pages"], cmp_dst[:, first * 256:], "cmp_in_po", 3)
                po.wait_ge(sem("proj_out"), BLK_KC * TILES + i + 1)
                dst = o[2][i * P:i * P + P] if i < PT else o[3]
                po.dma_start(dst, stk[0:rows, i % 4, :]).then_inc(sem("kvc_first" if i == 0 else "kvc_out"), 16)
            po.wait_ge(sem("cmp_mm"), 8)
            load_pages(po, PAGES, PAGES, t["sel_pages"], ring[:, SEL_SLOT[1], :], "sel_in1", 4)
            po.wait_ge(sem("proj_done"), 5 * TILES)
            load_pages(po, 3 * PAGES, PAGES, t["sel_pages"], ring[:, SEL_SLOT[3], :], "sel_in3", 4)
            for i in range(TILES):
                rows = ROWS[i]
                dst = o[4][i * P:i * P + P] if i < PT else o[5]
                po.dma_start(dst, kvn[0:rows, i, 0:256]).then_inc(sem("kv_out"), 16)
                po.wait_ge(sem("proj_out"), BLK_KW * TILES + i + 1)
                dst = o[6][i * P:i * P + P] if i < PT else o[7]
                po.dma_start(dst, kvn[0:rows, i, 256:512]).then_inc(sem("kv_out"), 16)
            po.wait_ge(sem("samp_pv"), 1)
            for q in (1, 3):
                load_pages(po, PAGES * (HALF + q), PAGES, t["sel_pages"], ring[:, SEL_SLOT[q], :], "sel_in%d" % q, 4)
            for i in range(TILES):
                rows = ROWS[i]
                po.wait_ge(sem("h2_ready"), i + 1)
                po.dma_start(scratch_h2[i * P:i * P + rows, :], h2[i % 2][0:rows, :]).then_inc(sem("h2_out%d" % (i % 2)), 16)
            po.wait_ge(sem("mix_used"), TILES)
            po.wait_ge(sem("attn_done"), 1)
            for k in range(2):
                nc.gpsimd.memset(xe[k], 0.0).then_inc(sem("xe_zero"), 1)
            po.wait_ge(sem("slots_empty"), 16)
            for k in range(2):
                po.wait_ge(sem("slots_ready"), k + 1)
                for i in range(TILES):
                    rows = ROWS[i]
                    po.indirect_dma_start(
                        scratch_ix, bass.IndirectOffsetOnAxis(ints[0:rows, 5 * k + i:5 * k + i + 1].bitcast(U32), 0),
                        ints[0:rows, 20 + i:21 + i], None).then_inc(sem("slots_out"), 16)
            po.wait_ge(sem("slots_out"), 16 * 2 * TILES)

            def slots_back(b):
                po.dma_start(slot_tokens[0:CAP, E * b:E * b + E],
                             scratch_ix[b * CAP * E:(b + 1) * CAP * E, :].rearrange("(s e) o -> s (e o)", e=E)
                             ).then_inc(sem("slots_back"), 16)

            slots_back(0)
            for k in range(2):
                po.wait_ge(sem("h2_out%d" % k), 16 * (3 - k))
            po.wait_ge(sem("slots_back"), 16)
            po.wait_ge(sem("xe_zero"), 2)

            last_token = po.to_reg(TOK - 1)

            def passes(b):
                def gather(e, par):
                    after(po, "xt_mm", b * E + e - 1)
                    nc.gpsimd.tensor_copy(ints[0:CAP, 82 + par:83 + par], slot_tokens[0:CAP, bass.ds(b * E + e, 1)])
                    po.drain()
                    po.indirect_dma_start(xe[par][0:CAP, :], None, scratch_h2,
                                          bass.IndirectOffsetOnAxis(ints[0:CAP, 82 + par:83 + par].bitcast(U32), 0),
                                          bounds_check=last_token, oob_is_err=False).then_inc(sem("xe_in%d" % par), 16)

                def y_store(e, par):
                    po.wait_ge(sem("y_out"), 2 * (b * E + e) + 2)
                    if isinstance(b, int):
                        dst = scratch_y[bass.ds(e * CAP, CAP), :]
                    else:
                        dst = scratch_z[bass.ds((e * (PASSES - 1) + b - 1) * CAP, CAP), :]
                    po.dma_start(dst, ye[par][0:CAP, :]).then_inc(sem("y_stored%d" % par), 16)

                gather(0, 0)
                gather(1, 1)
                gather(2, 0)
                y_store(0, 0)
                with po.Fori(1, E // 2 - 1) as m:
                    gather(2 * m + 1, 1)
                    y_store(2 * m - 1, 1)
                    gather(2 * m + 2, 0)
                    y_store(2 * m, 0)
                gather(E - 1, 1)
                for e in range(E - 3, E):
                    y_store(e, e % 2)

            def results(table, column, name):
                last_row = po.to_reg(table.shape[0] - 1)
                for i in range(TILES):
                    for k in range(2):
                        at = column + 5 * k + i
                        po.indirect_dma_start(
                            yg[2 * i + k][0:ROWS[i], :], None, table,
                            bass.IndirectOffsetOnAxis(ints[0:ROWS[i], at:at + 1].bitcast(U32), 0),
                            bounds_check=last_row, oob_is_err=False
                        ).then_inc(sem(name if name == "more_in" else name + str(i)), 16)

            passes(0)
            for k in range(2):
                po.wait_ge(sem("y_stored%d" % k), 16 * E // 2)
            po.wait_ge(sem("flag_ready"), 1)
            more = po.value_load(ints[0:1, 80:81], min_val=0, max_val=1)
            with po.If(more != 0):
                for b in range(1, PASSES):
                    slots_back(b)
                po.wait_ge(sem("slots_back"), 16 * PASSES)
                with po.Fori(1, PASSES) as b:
                    passes(b)
                for k in range(2):
                    po.wait_ge(sem("y_stored%d" % k), 16 * E // 2 * PASSES)
                results(scratch_z, 84, "more_in")
                po.wait_ge(sem("more_in"), 32 * TILES)
            po.sem_inc(sem("y_all"), 1)
            results(scratch_y, 10, "yg_in")
            po.wait_ge(sem("kvc_first"), 16)
            po.wait_ge(sem("kvc_out"), 16 * (TILES - 1))
            po.wait_ge(sem("kv_out"), 32 * TILES)
            po.wait_ge(sem("gmv_out"), 16)


def _layouts(inp):
    def a(name):
        return np.asarray(inp[name])

    x = np.concatenate([a("x_prompt")[0], a("x_sample").reshape(NS, D)], 0)
    consts, alibi, earlier = constants()
    cmp_kv = a("cache_cmp_kv")[0].reshape(NPOOL, 2, 32, 2, 2, G, HD)
    sel_kv = a("cache_sel_kv")[0].reshape(NPOOL, PAGE, 2, 2 * HD)
    win = a("state_win_kv")[0].reshape(NB, WIN, 2, 2 * HD)
    win_v = win[:, :, 1].reshape(NB, 4, P, P).transpose(0, 2, 1, 3).reshape(NB, P, 512)
    ws = a("w_spatial")[0]
    return {
        "x": x,
        "xT": x.T.reshape(KD, P, TOK).transpose(1, 0, 2).reshape(P, KD * TOK),
        "pages": a("page_table").astype(np.int32).reshape(1, P),
        "consts": consts, "alibi": alibi.reshape(P, 4096), "earlier": earlier,
        "pe": a("pe_cmp")[0].reshape(2, 32, 2, HD).transpose(2, 3, 0, 1).reshape(P, 2, 32),
        "w1": a("w_cmp1")[0].reshape(2, 32, P, P).transpose(2, 0, 1, 3).reshape(P, 2, SLOT),
        "w2": a("w_cmp2")[0].transpose(1, 0, 2),
        "g1": a("norm1_g")[0].reshape(KD, P).T, "gout": a("out_norm_g")[0].reshape(KD, P).T,
        "cmp_pages": cmp_kv.transpose(0, 3, 6, 4, 2, 5, 1).reshape(NPOOL, P, 256),
        "sel_pages": np.concatenate([sel_kv[:, :, 0].transpose(0, 2, 1), sel_kv[:, :, 1]], 2),
        "win": np.concatenate([win[:, :, 0].transpose(0, 2, 1), win_v], 2),
        "ln_g": a("gm_ln_g")[0].reshape(1, 512), "ln_b": a("gm_ln_b")[0].reshape(1, 512),
        "ws_t": ws.transpose(2, 0, 1).reshape(P, GM * P),
        "ws_s": np.tile(ws[:, :NT, :NT].transpose(2, 0, 1), (NB, 1, NB)).reshape(NS, GM * NS),
        "bs_t": a("b_spatial")[0].T, "bs_s": np.tile(a("b_spatial")[0][:, :NT].T, (NB, 1)),
        "w_in": a("w_in")[0], "w_out": a("w_out")[0],
        "w_router": np.concatenate([a("w_router_group")[0], a("w_router_expert")[0]], 1)
        .reshape(KD, P, 20).transpose(1, 0, 2).reshape(P, KD * 20),
        "b_router": np.concatenate([a("b_router_group")[0], a("b_router_expert")[0]]).reshape(1, 20),
        "g2": a("norm2_g")[0].reshape(1, D), "gf": a("final_norm_g").reshape(1, D),
        "w_gate": a("w_gate_e")[0].reshape(E, KD, P, EH).transpose(0, 2, 1, 3).reshape(E, P, SLOT),
        "w_up": a("w_up_e")[0].reshape(E, KD, P, EH).transpose(0, 2, 1, 3).reshape(E, P, SLOT),
        "w_down": a("w_down_e")[0].reshape(E, FE, P, D).transpose(0, 2, 1, 3).reshape(E, P, SLOT),
    }


_OUTS = [(SEQ, D), (NS, D)] + [(SEQ, 256), (NS, 256)] * 3 + [(NS, 512)]
_SHAPES = [(1, SEQ, D), (NB, NT, D)] + [(1, 1, SEQ, 2, G, HD), (1, NB, NT, 2, G, HD)] * 3 + [(1, NB, NT, GM, HD)]


def kernel(**inputs):
    import numpy as _np
    import concourse.bacc as _bacc
    from concourse import mybir as _mybir
    from concourse.bass_utils import run_bass_kernel_spmd as _run

    nc = _bacc.Bacc("TRN2", target_bir_lowering=False, num_devices=1)
    arrays, aps = {}, {}
    for name, a in _layouts(inputs).items():
        a = _np.ascontiguousarray(a)
        arrays[f"in_{name}_dram"] = a
        aps[name] = nc.dram_tensor(f"in_{name}_dram", a.shape, _mybir.dt.from_np(a.dtype), kind="ExternalInput").ap()
    outs = [nc.dram_tensor(f"out_{i}_dram", s, F32, kind="ExternalOutput").ap() for i, s in enumerate(_OUTS)]
    hybrid_layer(nc, aps, outs)
    r = _run(nc, [arrays], core_ids=[0])
    return tuple(r.results[0][f"out_{i}_dram"].reshape(s) for i, s in enumerate(_SHAPES))
```
